# Optimizing a Trainium2 kernel written in Bass

```python
import jax, jax.numpy as jnp
from jax import lax
import numpy as np

D_MODEL = 1024
BATCH = 1
SEQ = 2048
DEPTH = 2

N_MIXERS = 2
N_ATTN_LAYERS = (DEPTH + 1) // 2
N_REC_LAYERS = DEPTH // 2

HEAD_DIM = 64
N_HEADS = D_MODEL // HEAD_DIM
N_KV_HEADS = 2
GROUP = N_HEADS // N_KV_HEADS
ATTN_WIDTH = N_HEADS * HEAD_DIM
KV_WIDTH = N_KV_HEADS * HEAD_DIM
ATTN_IN = 2 * ATTN_WIDTH + 2 * KV_WIDTH
WINDOW = 128
ATTN_BLOCK = 128
ROPE_THETA = 500000.0
ROPE_DIM = HEAD_DIM // 4

REC_HEADS = 8
REC_KEY_DIM = 128
REC_VALUE_DIM = D_MODEL // REC_HEADS
FORGET_DIM = REC_HEADS * REC_KEY_DIM
REC_WIDTH = REC_HEADS * REC_VALUE_DIM
REC_IN = 2 * FORGET_DIM + 2 * REC_WIDTH
REC_CHUNK = 32

NORM_EPS = 1e-6


def rmsnorm(x, w):
    xf = x.astype(jnp.float32)
    y = xf * lax.rsqrt(jnp.mean(xf * xf, axis=-1, keepdims=True) + NORM_EPS)
    return (y * w.astype(jnp.float32)).astype(x.dtype)

def partial_rope(x, positions):
    half = ROPE_DIM // 2
    inv_freq = ROPE_THETA ** (-(jnp.arange(half, dtype=jnp.float32) * 2.0 / ROPE_DIM))
    ang = positions.astype(jnp.float32)[..., None] * inv_freq
    cos = jnp.cos(ang)[:, :, None, :]
    sin = jnp.sin(ang)[:, :, None, :]
    x1 = x[..., :half].astype(jnp.float32)
    x2 = x[..., half:ROPE_DIM].astype(jnp.float32)
    r1 = x1 * cos - x2 * sin
    r2 = x2 * cos + x1 * sin
    return jnp.concatenate([r1.astype(x.dtype), r2.astype(x.dtype), x[..., ROPE_DIM:]], axis=-1)

def sliding_window_gqa(q, k, v, sinks):
    B, T = q.shape[0], q.shape[1]
    nb = T // ATTN_BLOCK
    qb = q.reshape(B, nb, ATTN_BLOCK, N_KV_HEADS, GROUP, HEAD_DIM).transpose(1, 0, 2, 3, 4, 5)

    def span(t):
        tb = t.reshape(B, nb, ATTN_BLOCK, N_KV_HEADS, HEAD_DIM)
        prev = jnp.pad(tb, ((0, 0), (1, 0), (0, 0), (0, 0), (0, 0)))[:, :-1]
        return jnp.concatenate([prev, tb], axis=2).transpose(1, 0, 2, 3, 4)

    kk, vv = span(k), span(v)
    q_rel = jnp.arange(ATTN_BLOCK)[:, None] + ATTN_BLOCK
    k_rel = jnp.arange(2 * ATTN_BLOCK)[None, :]
    band = (k_rel <= q_rel) & (q_rel - k_rel < WINDOW)
    sink = sinks.astype(jnp.float32).reshape(N_KV_HEADS, GROUP)[None, :, :, None]
    scale = HEAD_DIM ** -0.5

    def block(args):
        qi, ki, vi, idx = args
        s = jnp.einsum('bqhgd,bkhd->bhgqk', qi, ki, preferred_element_type=jnp.float32) * scale
        valid = band & ((idx > 0) | (k_rel >= ATTN_BLOCK))
        s = jnp.where(valid, s, -jnp.inf)
        m = jnp.maximum(jnp.max(s, axis=-1), sink)
        p = jnp.exp(s - m[..., None])
        denom = jnp.sum(p, axis=-1) + jnp.exp(sink - m)
        p = (p / denom[..., None]).astype(vi.dtype)
        return jnp.einsum('bhgqk,bkhd->bqhgd', p, vi)

    out = lax.map(block, (qb, kk, vv, jnp.arange(nb)))
    return out.transpose(1, 0, 2, 3, 4, 5).reshape(B, T, ATTN_WIDTH)

def attention_mixer(h, positions, w_in, b_in, sinks, w_out, b_out):
    B, T = h.shape[0], h.shape[1]
    proj = h @ w_in + b_in
    q, k, v, z = jnp.split(proj, [ATTN_WIDTH, ATTN_WIDTH + KV_WIDTH, ATTN_WIDTH + 2 * KV_WIDTH], axis=-1)
    q = partial_rope(q.reshape(B, T, N_HEADS, HEAD_DIM), positions)
    k = partial_rope(k.reshape(B, T, N_KV_HEADS, HEAD_DIM), positions)
    v = v.reshape(B, T, N_KV_HEADS, HEAD_DIM)
    o = sliding_window_gqa(q, k, v, sinks)
    return (o * jax.nn.silu(z)) @ w_out + b_out

def chunked_gated_recurrence(q, k, v, log_f):
    B, T, H, K = q.shape
    V = v.shape[-1]
    nc = T // REC_CHUNK

    def to_chunks(t):
        return t.reshape(B, nc, REC_CHUNK, H, t.shape[-1]).transpose(1, 0, 3, 2, 4)

    qc, kc, vc, gc = to_chunks(q), to_chunks(k), to_chunks(v), to_chunks(log_f)
    causal = jnp.tril(jnp.ones((REC_CHUNK, REC_CHUNK), dtype=bool))[:, :, None]

    def step(S, inp):
        qi, ki, vi, gi = inp
        b = jnp.cumsum(gi, axis=2)
        b_last = b[:, :, -1:, :]
        o_inter = jnp.einsum('bhck,bhkv->bhcv', qi * jnp.exp(b), S)
        diff = b[:, :, :, None, :] - b[:, :, None, :, :]
        decay = jnp.exp(jnp.where(causal, diff, -jnp.inf))
        scores = jnp.einsum('bhtk,bhtsk->bhts', qi, decay * ki[:, :, None, :, :])
        o_intra = jnp.einsum('bhts,bhsv->bhtv', scores, vi)
        S_new = S * jnp.exp(b_last)[:, :, 0, :, None] + jnp.einsum(
            'bhck,bhcv->bhkv', ki * jnp.exp(b_last - b), vi)
        return S_new, o_inter + o_intra

    S0 = jnp.zeros((B, H, K, V), jnp.float32)
    _, o = lax.scan(step, S0, (qc, kc, vc, gc))
    return o.transpose(1, 0, 3, 2, 4).reshape(B, T, H, V)

def hgrn2_mixer(h, lower_bound, w_in, gnorm_w, w_out):
    B, T = h.shape[0], h.shape[1]
    proj = h @ w_in
    q, f, i, z = jnp.split(proj, [FORGET_DIM, 2 * FORGET_DIM, 2 * FORGET_DIM + REC_WIDTH], axis=-1)
    q = jax.nn.silu(q.astype(jnp.float32)).reshape(B, T, REC_HEADS, REC_KEY_DIM)
    lb = lower_bound.astype(jnp.float32)
    log_f = jnp.logaddexp(jnp.log(lb), jnp.log1p(-lb) + jax.nn.log_sigmoid(f.astype(jnp.float32)))
    k = -jnp.expm1(log_f)
    log_f = log_f.reshape(B, T, REC_HEADS, REC_KEY_DIM)
    k = k.reshape(B, T, REC_HEADS, REC_KEY_DIM)
    v = i.astype(jnp.float32).reshape(B, T, REC_HEADS, REC_VALUE_DIM)
    o = chunked_gated_recurrence(q, k, v, log_f)
    o = o * lax.rsqrt(jnp.mean(o * o, axis=-1, keepdims=True) + NORM_EPS) * gnorm_w.astype(jnp.float32)
    o = o.reshape(B, T, REC_WIDTH) * jax.nn.silu(z.astype(jnp.float32))
    return o.astype(h.dtype) @ w_out

def first_inputs(seed: int = 0) -> dict:
    key = jax.random.key(seed)
    ks = jax.random.split(key, 16)
    f32 = jnp.float32
    x = jax.random.normal(ks[0], (BATCH, SEQ, D_MODEL), f32)
    offsets = jax.random.randint(ks[1], (BATCH, 1), 0, 4096, dtype=jnp.int32)
    positions = offsets + jnp.arange(SEQ, dtype=jnp.int32)[None, :]
    pre_norm_w = 1.0 + 0.02 * jax.random.normal(ks[2], (DEPTH, D_MODEL), f32)
    post_norm_w = 1.0 + 0.02 * jax.random.normal(ks[3], (DEPTH, D_MODEL), f32)
    attn_w_in = jax.random.normal(ks[4], (N_ATTN_LAYERS, D_MODEL, ATTN_IN), f32) * D_MODEL ** -0.5
    attn_b_in = 0.02 * jax.random.normal(ks[5], (N_ATTN_LAYERS, ATTN_IN), f32)
    attn_sinks = 0.5 * jax.random.normal(ks[6], (N_ATTN_LAYERS, N_HEADS), f32)
    attn_w_out = jax.random.normal(ks[7], (N_ATTN_LAYERS, ATTN_WIDTH, D_MODEL), f32) * ATTN_WIDTH ** -0.5
    attn_b_out = 0.02 * jax.random.normal(ks[8], (N_ATTN_LAYERS, D_MODEL), f32)
    rec_w_in = jax.random.normal(ks[9], (N_REC_LAYERS, D_MODEL, REC_IN), f32) * D_MODEL ** -0.5
    rec_lb_logits = 0.5 * jax.random.normal(ks[10], (DEPTH, FORGET_DIM), f32)
    rec_gnorm_w = 1.0 + 0.02 * jax.random.normal(ks[11], (N_REC_LAYERS, REC_VALUE_DIM), f32)
    rec_w_out = jax.random.normal(ks[12], (N_REC_LAYERS, REC_WIDTH, D_MODEL), f32) * REC_WIDTH ** -0.5
    return {"x": x, "positions": positions, "pre_norm_w": pre_norm_w, "post_norm_w": post_norm_w,
            "attn_w_in": attn_w_in, "attn_b_in": attn_b_in, "attn_sinks": attn_sinks,
            "attn_w_out": attn_w_out, "attn_b_out": attn_b_out, "rec_w_in": rec_w_in,
            "rec_lb_logits": rec_lb_logits, "rec_gnorm_w": rec_gnorm_w, "rec_w_out": rec_w_out}

def first_block(x, positions, pre_norm_w, post_norm_w, attn_w_in, attn_b_in, attn_sinks,
              attn_w_out, attn_b_out, rec_w_in, rec_lb_logits, rec_gnorm_w, rec_w_out):
    probs = jax.nn.softmax(rec_lb_logits.astype(jnp.float32), axis=0)
    cum = jnp.cumsum(probs, axis=0)
    lower_bounds = cum - cum[0:1]
    for layer in range(DEPTH):
        h = rmsnorm(x, pre_norm_w[layer])
        j = layer // N_MIXERS
        if layer % N_MIXERS == 0:
            y = attention_mixer(h, positions, attn_w_in[j], attn_b_in[j], attn_sinks[j],
                                attn_w_out[j], attn_b_out[j])
        else:
            y = hgrn2_mixer(h, lower_bounds[layer], rec_w_in[j], rec_gnorm_w[j], rec_w_out[j])
        x = x + rmsnorm(y, post_norm_w[layer])
    return x


DEPTH_2 = 1

D_MIX = D_MODEL

GLA_HEADS = 4
GLA_DK = 64
GLA_DV = 128
GLA_KW = GLA_HEADS * GLA_DK
GLA_VW = GLA_HEADS * GLA_DV
GLA_GATE_RANK = 16
GLA_TAU = 16.0
GLA_CHUNK = 64

RWKV_HEAD = 64
RWKV_W = D_MIX - GLA_VW
RWKV_HEADS = RWKV_W // RWKV_HEAD
RWKV_DECAY_RANK = 64
RWKV_A_RANK = 64
RWKV_GN_EPS = 64e-5

GLA_SPLITS = (GLA_KW, GLA_KW, GLA_VW, GLA_GATE_RANK, GLA_VW)
RWKV_SHIFT_SPLITS = (RWKV_W, RWKV_W, RWKV_W, RWKV_DECAY_RANK, RWKV_A_RANK)
GLA_IN = sum(GLA_SPLITS)
RWKV_SHIFT_W = sum(RWKV_SHIFT_SPLITS)
RWKV_IN = RWKV_SHIFT_W + RWKV_W
IN_WIDTH = GLA_IN + RWKV_IN


def _split(t, sizes):
    idx = np.cumsum(np.array(sizes))[:-1].tolist()
    return jnp.split(t, idx, axis=-1)

def _rmsnorm(x, w):
    xf = x.astype(jnp.float32)
    y = xf * lax.rsqrt(jnp.mean(xf * xf, axis=-1, keepdims=True) + NORM_EPS)
    return (y * w.astype(jnp.float32)).astype(x.dtype)

def _gla_chunked(q, k, v, log_a):
    B, T, H, DK = q.shape
    DV = v.shape[-1]
    C = GLA_CHUNK
    N = T // C

    def to_chunks(t):
        return t.reshape(B, N, C, H, t.shape[-1]).transpose(1, 0, 3, 2, 4)

    qc, kc, vc, gc = to_chunks(q), to_chunks(k), to_chunks(v), to_chunks(log_a)
    b = jnp.cumsum(gc, axis=3)
    b_last = b[:, :, :, -1:, :]
    q_in = qc * jnp.exp(b)
    k_in = kc * jnp.exp(-b)
    k_st = kc * jnp.exp(b_last - b)
    causal = jnp.tril(jnp.ones((C, C), dtype=bool))
    scores = jnp.einsum('nbhid,nbhjd->nbhij', q_in, k_in)
    scores = jnp.where(causal, scores, 0.0)
    o_intra = jnp.einsum('nbhij,nbhjv->nbhiv', scores, vc)
    d_state = jnp.einsum('nbhjd,nbhjv->nbhdv', k_st, vc)
    chunk_decay = jnp.exp(b_last[:, :, :, 0, :])

    def step(S, inp):
        dS, dec = inp
        return S * dec[..., None] + dS, S

    S0 = jnp.zeros((B, H, DK, DV), jnp.float32)
    _, S_prev = lax.scan(step, S0, (d_state, chunk_decay))
    o_inter = jnp.einsum('nbhid,nbhdv->nbhiv', q_in, S_prev)
    o = o_intra + o_inter
    return o.transpose(1, 0, 3, 2, 4).reshape(B, T, H, DV)

def _rwkv7_scan(r, decay, k, v, kk, a):
    B, T, H, N = r.shape

    def step(S, inp):
        r_t, w_t, k_t, v_t, kk_t, a_t = inp
        sa = jnp.einsum('bhvk,bhk->bhv', S, -kk_t)
        S = (S * w_t[:, :, None, :]
             + sa[..., None] * (kk_t * a_t)[:, :, None, :]
             + v_t[..., None] * k_t[:, :, None, :])
        y = jnp.einsum('bhvk,bhk->bhv', S, r_t)
        return S, y

    xs = tuple(t.transpose(1, 0, 2, 3) for t in (r, decay, k, v, kk, a))
    S0 = jnp.zeros((B, H, N, N), jnp.float32)
    _, y = lax.scan(step, S0, xs)
    return y.transpose(1, 0, 2, 3)

def _hybrid_layer(x, norm_w, w_in, gla_gate_up, gla_gate_bias, gla_norm_w,
                  rwkv_mu, rwkv_w0, rwkv_w_up, rwkv_a0, rwkv_a_up, rwkv_k_k,
                  rwkv_k_a, rwkv_r_k, rwkv_ln_w, rwkv_ln_b, w_out):
    B, T, _ = x.shape
    f32 = jnp.float32
    h = _rmsnorm(x, norm_w)
    u = (h @ w_in).astype(f32)
    gla_u, rwkv_u = u[..., :GLA_IN], u[..., GLA_IN:]

    gq, gk, gv, glr, gg = _split(gla_u, GLA_SPLITS)
    log_a = jax.nn.log_sigmoid(glr @ gla_gate_up.astype(f32) + gla_gate_bias.astype(f32)) / GLA_TAU
    q = gq.reshape(B, T, GLA_HEADS, GLA_DK) * (GLA_DK ** -0.5)
    k = gk.reshape(B, T, GLA_HEADS, GLA_DK)
    v = gv.reshape(B, T, GLA_HEADS, GLA_DV)
    o = _gla_chunked(q, k, v, log_a.reshape(B, T, GLA_HEADS, GLA_DK))
    o = o * lax.rsqrt(jnp.mean(o * o, axis=-1, keepdims=True) + NORM_EPS) * gla_norm_w.astype(f32)
    gla_out = o.reshape(B, T, GLA_VW) * jax.nn.silu(gg)

    shifted_cols = rwkv_u[..., :RWKV_SHIFT_W]
    rg = rwkv_u[..., RWKV_SHIFT_W:]
    prev = jnp.pad(shifted_cols, ((0, 0), (1, 0), (0, 0)))[:, :-1]
    mixed = shifted_cols + (prev - shifted_cols) * rwkv_mu.astype(f32)
    r, rk, rv, wl, al = _split(mixed, RWKV_SHIFT_SPLITS)
    w = -jax.nn.softplus(-(rwkv_w0.astype(f32) + jnp.tanh(wl) @ rwkv_w_up.astype(f32))) - 0.5
    decay = jnp.exp(-jnp.exp(w))
    a = jax.nn.sigmoid(rwkv_a0.astype(f32) + al @ rwkv_a_up.astype(f32))
    kk = (rk * rwkv_k_k.astype(f32)).reshape(B, T, RWKV_HEADS, RWKV_HEAD)
    kk = kk / jnp.maximum(jnp.linalg.norm(kk, axis=-1, keepdims=True), 1e-12)
    rk = rk * (1.0 + (a - 1.0) * rwkv_k_a.astype(f32))
    hs = (B, T, RWKV_HEADS, RWKV_HEAD)
    r_h, k_h, v_h = r.reshape(hs), rk.reshape(hs), rv.reshape(hs)
    y = _rwkv7_scan(r_h, decay.reshape(hs), k_h, v_h, kk, a.reshape(hs))
    mu = jnp.mean(y, axis=-1, keepdims=True)
    var = jnp.mean(jnp.square(y - mu), axis=-1, keepdims=True)
    y = ((y - mu) * lax.rsqrt(var + RWKV_GN_EPS)).reshape(B, T, RWKV_W)
    y = y * rwkv_ln_w.astype(f32) + rwkv_ln_b.astype(f32)
    bonus = jnp.sum(r_h * k_h * rwkv_r_k.astype(f32), axis=-1, keepdims=True) * v_h
    rwkv_out = (y + bonus.reshape(B, T, RWKV_W)) * jax.nn.silu(rg)

    merged = jnp.concatenate([gla_out, rwkv_out], axis=-1).astype(x.dtype)
    return x + merged @ w_out

def second_inputs(seed: int = 0) -> dict:
    key = jax.random.key(seed)
    ks = jax.random.split(key, 20)
    n = jax.random.normal
    L = DEPTH_2
    return {
        "x": n(ks[0], (BATCH, SEQ, D_MODEL), jnp.float32),
        "norm_w": 1.0 + 0.05 * n(ks[1], (L, D_MODEL), jnp.float32),
        "w_in": n(ks[2], (L, D_MODEL, IN_WIDTH), jnp.float32) * D_MODEL ** -0.5,
        "gla_gate_up": n(ks[3], (L, GLA_GATE_RANK, GLA_KW), jnp.float32) * GLA_GATE_RANK ** -0.5,
        "gla_gate_bias": 0.1 * n(ks[4], (L, GLA_KW), jnp.float32),
        "gla_norm_w": 1.0 + 0.05 * n(ks[5], (L, GLA_DV), jnp.float32),
        "rwkv_mu": jax.random.uniform(ks[6], (L, RWKV_SHIFT_W), jnp.float32),
        "rwkv_w0": jax.random.uniform(ks[7], (L, RWKV_W), jnp.float32, -6.0, -1.0),
        "rwkv_w_up": 0.1 * n(ks[8], (L, RWKV_DECAY_RANK, RWKV_W), jnp.float32),
        "rwkv_a0": 0.1 * n(ks[9], (L, RWKV_W), jnp.float32),
        "rwkv_a_up": 0.1 * n(ks[10], (L, RWKV_A_RANK, RWKV_W), jnp.float32),
        "rwkv_k_k": 0.85 + 0.05 * n(ks[11], (L, RWKV_W), jnp.float32),
        "rwkv_k_a": 1.0 + 0.05 * n(ks[12], (L, RWKV_W), jnp.float32),
        "rwkv_r_k": 0.1 * n(ks[13], (L, RWKV_HEADS, RWKV_HEAD), jnp.float32),
        "rwkv_ln_w": 1.0 + 0.05 * n(ks[14], (L, RWKV_W), jnp.float32),
        "rwkv_ln_b": 0.02 * n(ks[15], (L, RWKV_W), jnp.float32),
        "w_out": n(ks[16], (L, D_MIX, D_MODEL), jnp.float32) * D_MIX ** -0.5,
        "final_norm_w": 1.0 + 0.05 * n(ks[17], (D_MODEL,), jnp.float32),
    }

def second_block(x, norm_w, w_in, gla_gate_up, gla_gate_bias, gla_norm_w, rwkv_mu,
              rwkv_w0, rwkv_w_up, rwkv_a0, rwkv_a_up, rwkv_k_k, rwkv_k_a,
              rwkv_r_k, rwkv_ln_w, rwkv_ln_b, w_out, final_norm_w):
    for l in range(DEPTH_2):
        x = _hybrid_layer(x, norm_w[l], w_in[l], gla_gate_up[l], gla_gate_bias[l],
                          gla_norm_w[l], rwkv_mu[l], rwkv_w0[l], rwkv_w_up[l],
                          rwkv_a0[l], rwkv_a_up[l], rwkv_k_k[l], rwkv_k_a[l],
                          rwkv_r_k[l], rwkv_ln_w[l], rwkv_ln_b[l], w_out[l])
    return _rmsnorm(x, final_norm_w)


def setup_inputs(seed=0):
    out = dict(first_inputs(seed))
    for name, value in second_inputs(seed + 1).items():
        if name != "x":
            out[name + "_2"] = value
    return out


def reference(
    x, positions, pre_norm_w, post_norm_w, attn_w_in, attn_b_in, attn_sinks, attn_w_out,
    attn_b_out, rec_w_in, rec_lb_logits, rec_gnorm_w, rec_w_out, norm_w_2, w_in_2,
    gla_gate_up_2, gla_gate_bias_2, gla_norm_w_2, rwkv_mu_2, rwkv_w0_2, rwkv_w_up_2, rwkv_a0_2,
    rwkv_a_up_2, rwkv_k_k_2, rwkv_k_a_2, rwkv_r_k_2, rwkv_ln_w_2, rwkv_ln_b_2, w_out_2,
    final_norm_w_2,
):
    x = first_block(
        x, positions, pre_norm_w, post_norm_w, attn_w_in, attn_b_in, attn_sinks, attn_w_out,
        attn_b_out, rec_w_in, rec_lb_logits, rec_gnorm_w, rec_w_out,
    )
    return second_block(
        x, norm_w_2, w_in_2, gla_gate_up_2, gla_gate_bias_2, gla_norm_w_2, rwkv_mu_2, rwkv_w0_2,
        rwkv_w_up_2, rwkv_a0_2, rwkv_a_up_2, rwkv_k_k_2, rwkv_k_a_2, rwkv_r_k_2, rwkv_ln_w_2,
        rwkv_ln_b_2, w_out_2, final_norm_w_2,
    )


_drawn_inputs = setup_inputs


def setup_inputs(seed=0):
    import zlib

    import numpy as np

    out = dict(_drawn_inputs(seed))
    spreads = {}
    factors = {'attn_sinks': 5.612,
     'rec_gnorm_w': 3.957,
     'gla_gate_bias_2': 4.971,
     'gla_norm_w_2': 4.459,
     'rwkv_w_up_2': 4.257,
     'rwkv_a0_2': 6.77,
     'rwkv_k_k_2': 4.081,
     'rwkv_k_a_2': 3.382,
     'rwkv_ln_w_2': 4.76,
     'rwkv_ln_b_2': 22.312}
    for name, (base, spread) in spreads.items():
        noise = np.random.default_rng([zlib.crc32(name.encode()), seed]).standard_normal(out[name].shape)
        drawn = base * np.exp(spread * noise) if base else spread * noise
        out[name] = __import__('jax').numpy.asarray(drawn.astype(out[name].dtype))
    for name, factor in factors.items():
        out[name] = (out[name] * factor).astype(out[name].dtype)
    return out
```

```python
from contextlib import ExitStack

import numpy as np
import concourse.bass as bass
from concourse import mybir

F32 = mybir.dt.float32
I32 = mybir.dt.int32
ACT = mybir.ActivationFunctionType
ALU = mybir.AluOpType
AX = mybir.AxisListType

P = 128
T = 2048
D = 1024
NT = T // P
KC = D // P
G = 512
NG = T // G
EPS = 1e-6
HD = 64
NH = 16
NKV = 2
GRP = NH // NKV
ROPE = HD // 4
RH = ROPE // 2
KV0 = NH * HD
V0 = KV0 + NKV * HD
Z0 = V0 + NKV * HD
QKV = Z0
RK = 128
LEVELS = 7
CH = 64
GLA_Q, GLA_K, GLA_V, GLA_R, GLA_Z = 0, 256, 512, 1024, 1040
RW = 1552
RW_R, RW_K, RW_V, RW_WA, RW_Z = RW, RW + 512, RW + 1024, RW + 1536, RW + 1664
GN_EPS = 64e-5
NEG = -1e30
NINE_LN2 = 9 * float(np.log(2.0))


VECTORS = {
    "pre0": ("pre_norm_w", 0, 8), "pre1": ("pre_norm_w", 1, 8), "norm2": ("norm_w_2", 0, 8),
    "att_b": ("attn_b_in", 0, 18), "lb0": ("rec_lb_logits", 0, 8), "lb1": ("rec_lb_logits", 1, 8),
    "rec_gn": ("rec_gnorm_w", 0, 1), "gla_b": ("gla_gate_bias_2", 0, 2), "gla_gn": ("gla_norm_w_2", 0, 1),
    "mu": ("rwkv_mu_2", 0, 13), "w0": ("rwkv_w0_2", 0, 4), "a0": ("rwkv_a0_2", 0, 4),
    "kk": ("rwkv_k_k_2", 0, 4), "ka": ("rwkv_k_a_2", 0, 4), "rk": ("rwkv_r_k_2", 0, 4),
    "lw": ("rwkv_ln_w_2", 0, 4), "lb": ("rwkv_ln_b_2", 0, 4),
}
COLUMNS, _at = {}, 0
for _name, (_, _, _n) in VECTORS.items():
    COLUMNS[_name] = (_at, _n)
    _at += _n
COLUMNS["att_zb"] = (COLUMNS["att_b"][0] + Z0 // P, D // P)
COLUMNS["rwkv"] = (COLUMNS["mu"][0], _at - COLUMNS["mu"][0])


def feature_columns(inputs):
    return np.ascontiguousarray(np.concatenate(
        [np.asarray(inputs[src])[row].reshape(-1, P).T for src, row, _ in VECTORS.values()], 1))


def constant_tables():
    s = np.arange(P)[:, None]
    t = np.arange(P)[None, :]
    i64, j64 = np.arange(P)[:, None] % CH, np.arange(CH)[None, :]
    parts = {"ident": (s == t)}
    prev, cur = np.where(t > s, 0.0, NEG), np.where(t <= s, 0.0, NEG)
    parts["band"] = np.concatenate([prev, cur], 1)
    col = np.arange(G)[None, :] + 0 * s
    parts["run128"] = (col % P != 0)
    parts["run64"] = (col % CH != 0)
    parts["gla"] = (s <= t) & (s // CH == t // CH)
    strict, incl = i64 < j64, i64 <= j64
    parts["delta"] = np.concatenate([strict, incl, strict, incl], 1)
    for l in range(6):
        h = 1 << l
        low = (i64 // (2 * h) == j64 // (2 * h)) & (i64 % (2 * h) >= h) & (j64 % (2 * h) < h)
        parts[f"low{l}"] = low
    parts["up0"] = (i64 // 2 == j64 // 2) & (i64 < j64)
    parts["eye64"] = (i64 == j64)
    parts["head_ones"] = (s // HD == t // HD)
    parts["ones"] = np.ones((P, P))
    cols, at, off = [], {}, 0
    for name, a in parts.items():
        a = np.ascontiguousarray(a, dtype=np.float32)
        at[name] = (off, a.shape[1])
        off += a.shape[1]
        cols.append(a)
    masks = []
    for l in range(LEVELS):
        h = 1 << l
        m = (s // (2 * h) == t // (2 * h)) & (s % (2 * h) < h)
        masks += [m[:, (np.arange(P) % (2 * h)) >= h]] * (G // P)
    select = np.concatenate(masks, 1).astype(np.float32)
    half = RH
    inv = np.float32(500000.0) ** (-(np.arange(half, dtype=np.float32) * np.float32(2.0) / np.float32(ROPE)))
    freq = np.tile(inv.astype(np.float32)[None, :], (P, NT))
    return np.concatenate(cols + [freq], 1), at | {"freq": (off, NT * half)}, select


def bc(ap, axis, n):
    a = ap.unsqueeze(axis)
    shape = list(a.shape)
    shape[axis] = n
    return a.broadcast_to(shape)


class Engine:

    def __init__(self, eng, sem):
        self.e, self.sem, self.n, self.seen = eng, sem, 0, {}

    def wait(self, *tokens):
        for sem, value in tokens:
            if self.seen.get(sem.num, 0) < value:
                self.seen[sem.num] = value
                self.e.wait_ge(sem, value)

    def inc(self, ins):
        self.n += 1
        ins.then_inc(self.sem, 1)
        return (self.sem, self.n)

    def tt(self, out, a, b, op, *w):
        self.wait(*w)
        return self.inc(self.e.tensor_tensor(out, a, b, op))

    def ts(self, out, a, s1, s2, op0, op1, *w):
        self.wait(*w)
        if s2 is None:
            return self.inc(self.e.tensor_scalar(out, a, s1, None, op0))
        return self.inc(self.e.tensor_scalar(out, a, s1, s2, op0, op1))

    def stt(self, out, a, s, b, op0, op1, *w):
        self.wait(*w)
        return self.inc(self.e.scalar_tensor_tensor(out=out, in0=a, scalar=s, in1=b, op0=op0, op1=op1))

    def copy(self, out, a, *w):
        self.wait(*w)
        return self.inc(self.e.tensor_copy(out, a))

    def act(self, out, a, f, *w, bias=0.0, scale=1.0, accum=None):
        self.wait(*w)
        if accum is None:
            return self.inc(self.e.activation(out, a, f, bias=bias, scale=scale))
        return self.inc(self.e.activation(out, a, f, bias=bias, scale=scale, accum_out=accum))


class Slot:

    def __init__(self, ap):
        self.ap, self.free = ap, ()


class Ring:

    def __init__(self, aps):
        self.slots, self.i = [Slot(a) for a in aps], 0

    def take(self):
        s = self.slots[self.i % len(self.slots)]
        self.i += 1
        assert s.free is not None, "taken again before its readers are known"
        s.was, s.free = s.free, None
        return s


class Dma:

    def __init__(self, new_sem):
        self.new_sem, self.count, self.stores = new_sem, {}, []

    def start(self, eng, key, out, in_, *w, store=False):
        eng.wait(*w)
        if key not in self.count:
            self.count[key] = [self.new_sem(f"dma_{key}"), 0]
        c = self.count[key]
        c[1] += 16
        eng.e.dma_start(out, in_).then_inc(c[0], 16)
        if store:
            self.stores.append((c[0], c[1]))
        return (c[0], c[1])


STEPS = {}


def interleave(*streams):
    live = [[name, gen, 0, STEPS.get(name, 20)] for name, gen in streams if gen is not None]
    while live:
        s = min(live, key=lambda s: s[2] / s[3])
        if next(s[1], "end") == "end":
            STEPS[s[0]] = max(s[2], 1)
            live.remove(s)
        s[2] += 1


class Core:

    def __init__(self, nc, ctx, ins, at):
        self.nc, self.ctx, self.ins, self.table = nc, ctx, ins, None
        sem = lambda n: ctx.enter_context(nc.semaphore(n))
        self.pe = Engine(nc.tensor, sem("pe_done"))
        self.act = Engine(nc.scalar, sem("act_done"))
        self.dve = Engine(nc.vector, sem("dve_done"))
        self.pool = Engine(nc.gpsimd, sem("pool_done"))
        self.sp = Engine(nc.sync, sem("sp_done"))
        self.dma = Dma(sem)
        self.bank = [ctx.enter_context(nc.psum_tensor(f"bank{i}", [P, 512], F32)) for i in range(8)]
        sb = lambda n, w, dt=F32: ctx.enter_context(nc.sbuf_tensor(n, [P, w], dt))
        self.hT = sb("hT", KC * T)[:, :].rearrange("p (c t) -> p c t", c=KC)
        self.oT = sb("oT", KC * T)[:, :].rearrange("p (c t) -> p c t", c=KC)
        self.cst_w = max(o + w for o, w in at.values())
        self.cst = sb("cst", self.cst_w)
        self.sel = sb("sel", LEVELS * G // 2, mybir.dt.int8)
        self.at = at
        self.columns = sb("feature_cols", COLUMNS["lb"][0] + COLUMNS["lb"][1])
        self.eps_at = {e: i for i, e in enumerate((EPS, 4 * EPS, GN_EPS, NINE_LN2, 1.0))}
        self.eps = sb("eps", 8)
        for e, i in self.eps_at.items():
            self.pool.inc(nc.gpsimd.memset(self.eps[:, i:i + 1], e))
        self.arena_words = 21020
        self.arena = sb("arena", self.arena_words)
        self.used = 0

    def c(self, name):
        o, w = self.at[name]
        return self.cst[:, o:o + w]

    def eps_col(self, e):
        i = self.eps_at[e]
        return self.eps[:, i:i + 1]

    def sel_queries(self, l):
        o = l * G // 2
        return self.sel[:, o:o + G // 2].rearrange("p (n i) -> p n i", i=1 << l)

    def room(self, words):
        a = self.arena[:, self.used:self.used + words]
        self.used += words
        assert self.used <= self.arena_words, self.used
        return a

    def new_phase(self):
        every = [(e.sem, e.n) for e in (self.pe, self.act, self.dve, self.pool) if e.n]
        every += [(c[0], c[1]) for c in self.dma.count.values()]
        for e in (self.pe, self.act, self.dve, self.pool, self.sp):
            e.wait(*every)
        self.used, self.table = 0, None
        return Ring([b[:, :] for b in self.bank])

    def load(self, key, out, in_, *w):
        return self.dma.start(self.sp, key, out, in_, *w)

    def load_constants(self, table, select):
        self.load("cst", self.cst[:, :], table)
        wide = self.oT[:, 0, 0:LEVELS * G // 2]
        got = self.load("sel", wide, select)
        self.dve.copy(self.sel[:, :], wide, got)
        self.columns_ready = self.load("columns", self.columns[:, :], self.ins["columns"])

    def weights(self, name, w, c0, n):
        return w[:, c0:c0 + n].rearrange("(c p) n -> p c n", p=P)

    def vec(self, key, out, name):
        o, w = COLUMNS[name]
        return self.dve.copy(out, self.columns[:, o:o + w], self.columns_ready)

    def row(self, key, out, src):
        n = src.shape[0]
        return self.load(key, out, src.unsqueeze(0).broadcast_to([P, n]))

    def project(self, bank, w, col, g, *waits, m=P, width=G):
        pe = self.pe
        pe.wait(*waits, *bank.was)
        for c in range(KC):
            ins = self.nc.tensor.matmul(bank.ap[0:m, 0:width], w[:, c, col:col + m],
                                        self.hT[:, c, g * width:(g + 1) * width], start=(c == 0), stop=(c == KC - 1))
            if c % 2 and c < KC - 1:
                yield
        return pe.inc(ins)

    def project_now(self, *args, **kw):
        gen = self.project(*args, **kw)
        while True:
            try:
                next(gen)
            except StopIteration as end:
                return end.value

    def ln(self, out, a, *w, **kw):
        if self.table != "ln":
            self.nc.scalar.preload_act_table_set("natural_log_exp_and_others")
            self.table = "ln"
        return self.act.act(out, a, ACT.Ln, *w, **kw)

    def tanh(self, out, a, *w, **kw):
        self.table = "tanh"
        return self.act.act(out, a, ACT.Tanh, *w, **kw)

    def norm_rows(self, x, junk, st, n, *w):
        a, v = self.act, self.dve
        t = a.act(junk, x, ACT.Square, *w, accum=st[:, n:n + 1])
        t = v.ts(st[:, n + 1:n + 2], st[:, n:n + 1], 1.0 / D, EPS, ALU.mult, ALU.add, t)
        t = a.act(st[:, n + 1:n + 2], st[:, n + 1:n + 2], ACT.Sqrt, t)
        v.wait(t)
        return v.inc(self.nc.vector.reciprocal(st[:, n + 2:n + 3], st[:, n + 1:n + 2]))

    def to_hT(self, psum, h, tile, nw, *w):
        pe, v = self.pe, self.dve
        wrote = []
        for half in range(2):
            b = psum.take()
            pe.wait(*w, *b.was)
            for j in range(4):
                c = 4 * half + j
                ins = self.nc.tensor.transpose(b.ap[:, j * P:(j + 1) * P], h[:, c * P:(c + 1) * P], self.c("ident"))
            t = pe.inc(ins)
            t2 = v.tt(self.hT[:, 4 * half:4 * half + 4, tile * P:(tile + 1) * P],
                      b.ap.rearrange("p (c t) -> p c t", c=4),
                      bc(nw[:, 4 * half:4 * half + 4], 2, P), ALU.mult, t)
            b.free = (t2,)
            wrote.append(t2)
        return t, wrote[-1]


def first_norm(k):
    psum = k.new_phase()
    xs = [k.room(D) for _ in range(2)]
    hs = [k.room(D) for _ in range(2)]
    nw, st = k.room(KC), k.room(8)
    nw_ready = k.vec("nw", nw, "pre0")
    xr, hr = Ring(xs), Ring(hs)
    for t in range(NT):
        x, h = xr.take(), hr.take()
        got = k.load(f"x{t % 2}", x.ap, k.ins["x"][0, t * P:(t + 1) * P, :], *x.was)
        r = k.norm_rows(x.ap, h.ap, st, 4 * (t % 2), got, *h.was, *((last[t - 2],) if t >= 2 else ()))
        scaled = k.dve.ts(h.ap, x.ap, st[:, 4 * (t % 2) + 2:4 * (t % 2) + 3], None, ALU.mult, None, r)
        x.free = (scaled,)
        if t == 0:
            last = []
            k.dve.wait(nw_ready)
        last.append(scaled)
        read, _ = k.to_hT(psum, h.ap, t, nw, scaled)
        h.free = (read,)


def finish_layer(k, layer, x_in, x_out, w_out, bias, post_w, next_w, last_w):
    psum = k.new_phase()
    v, a, pe = k.dve, k.act, k.pe
    wo = k.room(KC * D).rearrange("p (c n) -> p c n", c=KC)
    got_w = [k.load(f"wo{c}", wo[:, c, :], w_out[c * P:(c + 1) * P, :]) for c in range(KC)]
    ready = []
    if bias is not None:
        b_row = k.room(D)
        ready.append(k.row("b_row", b_row, bias))
    if post_w is not None:
        p_row = k.room(D)
        ready.append(k.row("p_row", p_row, post_w))
    if last_w is not None:
        l_row = k.room(D)
        ready.append(k.row("l_row", l_row, last_w))
    if next_w is not None:
        nw = k.room(KC)
        ready.append(k.vec("nw", nw, next_w))
    xr = Ring([k.room(D) for _ in range(2)])
    yr = Ring([k.room(D) for _ in range(2)])
    jr = Ring([k.room(D) for _ in range(2)])
    st = k.room(16)
    v.wait(*ready)

    def tile(t):
        x = xr.take()
        got = k.load(f"x{t % 2}", x.ap, x_in[t * P:(t + 1) * P, :], *x.was)
        s0 = 8 * (t % 2)
        y, junk = yr.take(), jr.take()
        done = []
        for n in range(2):
            b = psum.take()
            pe.wait(*b.was)
            for c in range(KC):
                pe.wait(got_w[c])
                ins = k.nc.tensor.matmul(b.ap, k.oT[:, c, t * P:(t + 1) * P], wo[:, c, n * 512:(n + 1) * 512],
                                         start=(c == 0), stop=(c == KC - 1))
            mm = pe.inc(ins)
            ysl = y.ap[:, n * 512:(n + 1) * 512]
            if bias is not None:
                b.free = (v.tt(ysl, b.ap, b_row[:, n * 512:(n + 1) * 512], ALU.add, mm, *y.was),)
            else:
                b.free = (a.act(ysl, b.ap, ACT.Copy, mm, *y.was),)
            done += b.free
        yield
        if post_w is not None:
            r = k.norm_rows(y.ap, junk.ap, st, s0, *done, *junk.was)
            scaled = v.stt(y.ap, y.ap, st[:, s0 + 2:s0 + 3], p_row, ALU.mult, ALU.mult, r)
        else:
            scaled = done[-1]
            v.wait(*done, *junk.was)
        new = v.tt(x.ap, x.ap, y.ap, ALU.add, scaled, got)
        yield
        r = k.norm_rows(x.ap, y.ap, st, s0 + 4, new)
        if last_w is not None:
            o = v.stt(junk.ap, x.ap, st[:, s0 + 6:s0 + 7], l_row, ALU.mult, ALU.mult, r, *junk.was)
            stored = k.dma.start(k.sp, f"out{t % 2}", x_out[t * P:(t + 1) * P, :], junk.ap, o, store=True)
            x.free, y.free, junk.free = (o,), (r,), (stored,)
            yield
            return
        stored = k.dma.start(k.sp, f"out{t % 2}", x_out[t * P:(t + 1) * P, :], x.ap, new, store=True)
        o = v.ts(junk.ap, x.ap, st[:, s0 + 6:s0 + 7], None, ALU.mult, None, r)
        yield
        read, _ = k.to_hT(psum, junk.ap, t, nw, o)
        x.free, y.free, junk.free = (o, stored), (r,), (read,)

    pending = None
    for t in range(NT):
        g = tile(t)
        next(g)
        if pending is not None:
            for _ in pending:
                pass
        pending = g
    for _ in pending:
        pass


def rope_tables(k, cos, sin, tmp, pos_i):
    v, a = k.dve, k.act
    got = k.load("pos", pos_i, k.ins["positions"])
    n = NT * RH
    pos, ang, turn, red = (tmp[:, i * n:(i + 1) * n] for i in range(4))
    t = v.copy(pos[:, 0:NT], pos_i, got)
    t = v.tt(ang.rearrange("p (n f) -> p n f", f=RH), k.c("freq").rearrange("p (n f) -> p n f", f=RH),
             bc(pos[:, 0:NT], 2, RH), ALU.mult, t)
    two_pi = 2.0 * np.pi
    hi = float(np.float32(6.28125))
    mid = float(np.round((two_pi - hi) * 2.0 ** 20) / 2.0 ** 20)
    low = float(two_pi - hi - mid)
    magic = float(1.5 * 2.0 ** 23)
    for out, quarter in ((sin, 0.0), (cos, 0.25)):
        t = v.ts(turn, ang, float(1.0 / two_pi), quarter, ALU.mult, ALU.add, t)
        t = v.ts(turn, turn, magic, -magic, ALU.add, ALU.add, t)
        t = v.stt(red, turn, -hi, ang, ALU.mult, ALU.add, t)
        t = v.stt(red, turn, -mid, red, ALU.mult, ALU.add, t)
        t = v.stt(red, turn, -low, red, ALU.mult, ALU.add, t)
        t = v.ts(red, red, float(quarter * two_pi), float(np.float32(np.pi) - np.float32(1e-6)), ALU.add, ALU.min, t)
        t = v.ts(red, red, -float(np.float32(np.pi) - np.float32(1e-6)), None, ALU.max, None, t)
        t = a.act(out, red, ACT.Sin, t)
    return t


def attention(k):
    psum = k.new_phase()
    v, a, pe, pool = k.dve, k.act, k.pe, k.pool
    nc = k.nc
    w_in = k.ins["attn_w_in"][0]
    wq = k.room(KC * QKV).rearrange("p (c n) -> p c n", c=KC)
    got_w = k.load("wq", wq, w_in[:, 0:QKV].rearrange("(c p) n -> p c n", p=P))
    b_row = k.room(QKV)
    got_b = k.row("b_row", b_row, k.ins["attn_b_in"][0, 0:QKV])
    sinks = k.room(NH)
    got_s = k.row("sinks", sinks, k.ins["attn_sinks"][0])
    cs, sn = k.room(NT * RH), k.room(NT * RH)
    tables = rope_tables(k, cs, sn, k.oT[:, 7, :], k.oT[:, 6, 0:NT].bitcast(I32))
    csv, snv = (x.rearrange("p (n f) -> p n f", f=RH) for x in (cs, sn))
    k_pair = [k.room(NKV * 2 * P).rearrange("p (g s t) -> p g s t", g=NKV, s=2) for _ in range(2)]
    v_keep = k.room(3 * P).rearrange("p (n d) -> p n d", n=3)
    qkv = Ring([k.room(QKV) for _ in range(1)])
    kd = Ring([k.room(2 * P)])
    ab = k.room(2 * 18 * ROPE)
    qT = Ring([k.room(8 * P) for _ in range(1)])
    prob = Ring([k.room(GRP * 2 * P)])
    probT = Ring([k.room(GRP * 2 * P)])
    st = k.room(6 * GRP)
    mx, ng, rs, se, dn, rc = (st[:, i * GRP:(i + 1) * GRP] for i in range(6))
    v.wait(got_b, got_s, tables)
    last = {"scores": (), "pv": (), "stat": ()}
    made = {}

    def qkv_tile(t):
        x = qkv.take()
        done = []
        for c0, n in ((0, 512), (512, 512), (1024, 256)):
            b = psum.take()
            pe.wait(got_w, *b.was)
            for c in range(KC):
                ins = nc.tensor.matmul(b.ap[:, 0:n], k.hT[:, c, t * P:(t + 1) * P], wq[:, c, c0:c0 + n],
                                       start=(c == 0), stop=(c == KC - 1))
            mm = pe.inc(ins)
            d = v.tt(x.ap[:, c0:c0 + n], b.ap[:, 0:n], b_row[:, c0:c0 + n], ALU.add, mm, *x.was)
            b.free = (d,)
            done.append(d)
            yield
        vv = a.act(v_keep[:, t % 3, :], x.ap[:, V0:V0 + P], ACT.Copy, *done, *last["pv"])
        heads = x.ap[:, 0:V0].rearrange("p (h d) -> p h d", d=HD)
        x12 = heads[:, :, 0:ROPE].rearrange("p h (a f) -> p h a f", a=2)
        pa = ab[:, 0:18 * ROPE].rearrange("p (h a f) -> p h a f", a=2, f=RH)
        pb = ab[:, 18 * ROPE:].rearrange("p (h a f) -> p h a f", a=2, f=RH)
        cb = bc(csv[:, t, :], 1, 18)
        sb = bc(snv[:, t, :], 1, 18)
        for i in range(2):
            ta = v.tt(pa[:, :, i, :], x12[:, :, i, :], cb, ALU.mult, *done)
            tb = v.tt(pb[:, :, i, :], x12[:, :, i, :], sb, ALU.mult)
        r1 = v.tt(x12[:, :, 0, :], pa[:, :, 0, :], pb[:, :, 1, :], ALU.subtract, tb)
        r2 = v.tt(x12[:, :, 1, :], pa[:, :, 1, :], pb[:, :, 0, :], ALU.add, tb)
        kk = kd.take()
        dup = v.copy(kk.ap.rearrange("p (g r d) -> p g r d", g=2, r=2),
                     bc(x.ap[:, KV0:KV0 + P].rearrange("p (g d) -> p g d", g=2), 2, 2),
                     r2, *kk.was)
        yield
        q = qT.take()
        outs = []
        for half in range(2):
            b = psum.take()
            pe.wait(r2, *b.was)
            for j in range(4):
                blk = 4 * half + j
                ins = nc.tensor.transpose(b.ap[:, j * P:(j + 1) * P], x.ap[:, blk * P:(blk + 1) * P], k.c("ident"))
            tr = pe.inc(ins)
            o = a.act(q.ap[:, half * 512:(half + 1) * 512], b.ap, ACT.Copy, tr, *q.was)
            b.free = (o,)
            outs.append(o)
        b = psum.take()
        pe.wait(dup, *b.was)
        for g in range(2):
            ins = nc.tensor.transpose(b.ap[:, g * P:(g + 1) * P], kk.ap[:, g * P:(g + 1) * P], k.c("ident"))
        tr = pe.inc(ins)
        kv = b.ap[:, 0:2 * P].rearrange("p (g t) -> p g t", g=2)
        o = a.act(k_pair[t % 2][:, :, 1, :], kv, ACT.Copy, tr, *last["scores"])
        o = a.act(k_pair[(t + 1) % 2][:, :, 0, :], kv, ACT.Copy)
        b.free = (o,)
        kk.free = (tr,)
        x.free = (vv, tr)
        made[t] = (q, outs[-1], o, vv)
        yield

    def attend(t):
        q, q_ready, k_ready, v_ready = made[t]
        lo = P if t == 0 else 0
        for g in range(NKV):
            p = prob.take()
            pv4 = p.ap.rearrange("p (h w) -> p h w", h=GRP)
            maxes = []
            for quad in range(2):
                banks = [psum.take(), psum.take()]
                pe.wait(q_ready, k_ready, *banks[0].was, *banks[1].was)
                for j in range(2):
                    for par in range(2):
                        blk = 4 * g + 2 * quad + j
                        rows = slice(64 * par, 64 * par + 64)
                        ins = nc.tensor.matmul(banks[par].ap[:, j * 256 + lo:(j + 1) * 256],
                                               q.ap[rows, blk * P:(blk + 1) * P],
                                               k_pair[t % 2][rows, g, lo // P:2, :], start=True, stop=True)
                mm = pe.inc(ins)
                last["scores"] = (mm,)
                for j in range(2):
                    for par in range(2):
                        h = 4 * quad + 2 * j + par
                        v.wait(mm, *p.was, *last["stat"])
                        m = v.inc(nc.vector.tensor_tensor_reduce(
                            out=pv4[:, h, lo:], in0=banks[par].ap[:, j * 256 + lo:(j + 1) * 256],
                            in1=k.c("band")[:, lo:], scale=HD ** -0.5, scalar=sinks[:, GRP * g + h:GRP * g + h + 1],
                            op0=ALU.add, op1=ALU.max, accum_out=mx[:, h:h + 1]))
                banks[0].free = banks[1].free = (m,)
                yield
            n1 = v.ts(ng, mx, -1.0, None, ALU.mult, None, m)
            n2 = v.tt(se, sinks[:, GRP * g:GRP * (g + 1)], mx, ALU.subtract, m)
            for h in range(GRP):
                e = a.act(pv4[:, h, lo:], pv4[:, h, lo:], ACT.Exp, n1, bias=ng[:, h:h + 1], accum=rs[:, h:h + 1])
            e2 = a.act(se, se, ACT.Exp, n2)
            d = v.tt(dn, rs, se, ALU.add, e, e2)
            v.wait(d)
            d = v.inc(nc.vector.reciprocal(rc, dn))
            for h in range(GRP):
                d = v.ts(pv4[:, h, lo:], pv4[:, h, lo:], rc[:, h:h + 1], 0.5, ALU.mult, ALU.mult, d if h == 0 else e)
            last["stat"] = (d,)
            yield
            pt = probT.take()
            ptv = pt.ap.rearrange("p (s h q) -> p s h q", s=2, h=GRP)
            evs = []
            for s in range(0 if t else 1, 2):
                for quad in range(2):
                    b = psum.take()
                    pe.wait(d, *b.was)
                    for j in range(4):
                        ins = nc.tensor.transpose(b.ap[:, j * P:(j + 1) * P],
                                                  pv4[:, 4 * quad + j, s * P:(s + 1) * P], k.c("ident"))
                    tr = pe.inc(ins)
                    o = a.act(ptv[:, s, 4 * quad:4 * quad + 4, :], b.ap.rearrange("p (h q) -> p h q", h=4),
                              ACT.Copy, tr, *pt.was)
                    b.free = (o,)
                    evs.append(o)
            p.free = (tr,)
            yield
            b = psum.take()
            pe.wait(*evs, v_ready, *b.was)
            pair = ptv.rearrange("p s (j r) q -> p s r j q", r=2)
            for par in range(2):
                for s in range(0 if t else 1, 2):
                    ins = nc.tensor.matmul(b.ap[64 * par:64 * par + 64, :], v_keep[:, (t - 1 + s) % 3, g * HD:(g + 1) * HD],
                                           pair[:, s, par, :, :], start=(s == (0 if t else 1)), stop=(s == 1))
            mm = pe.inc(ins)
            last["pv"] = (mm,)
            o = v.copy(k.oT[:, 4 * g:4 * g + 4, t * P:(t + 1) * P], b.ap.rearrange("p (j q) -> p j q", j=4), mm)
            b.free = (o,)
            pt.free = (mm,)
            yield
        q.free = (mm,)

    for _ in qkv_tile(0):
        pass
    for t in range(NT):
        if t + 1 < NT:
            g1, g2 = attend(t), qkv_tile(t + 1)
            for _ in range(4):
                next(g2)
                next(g1)
            for _ in g1:
                pass
            for _ in g2:
                pass
        else:
            for _ in attend(t):
                pass


def attention_gate(k):
    psum = k.new_phase()
    v, a = k.dve, k.act
    w_in = k.ins["attn_w_in"][0]
    wz = Ring([k.room(KC * P) for _ in range(3)])
    th = Ring([k.room(G) for _ in range(2)])
    u = Ring([k.room(G) for _ in range(2)])
    zb, hb = k.room(KC), k.room(KC)
    b = k.vec("zb", zb, "att_zb")
    half = v.ts(hb, zb, 0.5, None, ALU.mult, None, b)
    for f in range(KC):
        w = wz.take()
        wv = w.ap.rearrange("p (c n) -> p c n", c=KC)
        got = k.load(f"wz{f % 3}", wv, k.weights("z", w_in, Z0 + f * P, P), *w.was)
        for g in range(NG):
            bk, tb, ub = psum.take(), th.take(), u.take()
            mm = k.project_now(bk, wv, 0, g, got)
            t1 = k.tanh(tb.ap, bk.ap, mm, half, *tb.was, bias=hb[:, f:f + 1], scale=0.5)
            o = k.oT[:, f, g * G:(g + 1) * G]
            t2 = v.stt(ub.ap, bk.ap, zb[:, f:f + 1], o, ALU.add, ALU.mult, t1, *ub.was)
            t3 = v.stt(o, tb.ap, 1.0, ub.ap, ALU.add, ALU.mult, t1, t2)
            bk.free, tb.free, ub.free = (t2,), (t3,), (t3,)
        w.free = (mm,)


def recurrence(k):
    psum = k.new_phase()
    front_banks, back_banks = Ring([s.ap for s in psum.slots[0:3]]), Ring([s.ap for s in psum.slots[3:8]])
    v, a, pe, pool, nc = k.dve, k.act, k.pe, k.pool, k.nc
    w_in = k.ins["rec_w_in"][0]
    heads = D // RK
    wr = Ring([k.room(4 * KC * RK) for _ in range(2)])
    two = lambda: Ring([k.room(G) for _ in range(2)])
    one = lambda: Ring([k.room(G)])
    q_r, k_r, b_r, z_r, v_r = two(), two(), two(), two(), two()
    th_r, tf_r = two(), one()
    lg_r = one()
    d_r, e_r = two(), two()
    st_r = one()
    eb_r, qt_r, kt_r = one(), one(), one()
    sq_r, rs_r = e_r, d_r
    state = Ring([k.room(RK) for _ in range(6)])
    lb = k.room(8 * KC)
    l0, l1, lm, bb, ab, nb = (lb[:, i * KC:(i + 1) * KC] for i in range(6))
    gn = k.room(1)
    t0 = k.vec("lb0", l0, "lb0")
    t1 = k.vec("lb1", l1, "lb1")
    t2 = k.vec("gn", gn, "rec_gn")
    g_half = v.ts(gn, gn, 0.5, None, ALU.mult, None, t2)
    m = v.tt(lm, l0, l1, ALU.max, t0, t1)
    x0 = v.tt(l0, l0, lm, ALU.subtract, m)
    x1 = v.tt(l1, l1, lm, ALU.subtract, m)
    x0 = a.act(l0, l0, ACT.Exp, x0)
    x1 = a.act(l1, l1, ACT.Exp, x1)
    m = v.tt(lm, l0, l1, ALU.add, x0, x1)
    v.wait(m)
    m = v.inc(nc.vector.reciprocal(lm, lm))
    x1 = v.tt(l1, l1, lm, ALU.mult, m)
    x2 = v.ts(bb, l1, -0.5, 0.5, ALU.mult, ALU.add, x1)
    x3 = v.ts(nb, bb, -1.0, None, ALU.mult, None, x2)
    x4 = v.ts(ab, l1, 1e-7, None, ALU.max, None, x1)
    bounds = v.tt(ab, ab, bb, ALU.add, x4, x2)
    v.wait(x3)
    made = {}

    def load_head(h):
        w = wr.take()
        wv = w.ap.rearrange("p (i c n) -> p i c n", i=4, c=KC)
        got = [k.load(f"wr{h % 2}", wv[:, i], k.weights("", w_in, i * D + h * RK, RK), *w.was) for i in range(4)]
        return w, wv, got[-1]

    def front(h, g, w):
        slot, wv, got = w
        q, z = q_r.take(), z_r.take()
        pairs = []
        for i, dst in ((0, q), (3, z)):
            bank, th = front_banks.take(), th_r.take()
            mm = yield from k.project(bank, wv[:, i], 0, g, got)
            yield
            pairs.append((bank, th, dst, mm))
        bf, tf = front_banks.take(), tf_r.take()
        mf = yield from k.project(bf, wv[:, 1], 0, g)
        oks = []
        for bank, th, dst, mm in pairs:
            t = k.tanh(th.ap, bank.ap, mm, *th.was, scale=0.5)
            ok = v.stt(dst.ap, th.ap, 1.0, bank.ap, ALU.add, ALU.mult, t, *dst.was)
            bank.free, th.free = (ok,), (ok,)
            oks.append(ok)
        q_ok, z_ok = oks
        kk, lg, b = k_r.take(), lg_r.take(), b_r.take()
        t = k.tanh(tf.ap, bf.ap, mf, *tf.was, scale=0.5)
        bf.free = (t,)
        k_ok = v.ts(kk.ap, tf.ap, nb[:, h:h + 1], bb[:, h:h + 1], ALU.mult, ALU.add, t, bounds, *kk.was)
        t = k.ln(lg.ap, tf.ap, t, bounds, *lg.was, bias=ab[:, h:h + 1], scale=bb[:, h:h + 1])
        tf.free = (t, k_ok)
        v.wait(t, *b.was)
        b_ok = v.inc(nc.vector.tensor_tensor_scan(out=b.ap, data0=k.c("run128"), data1=lg.ap, initial=0.0,
                                                  op0=ALU.mult, op1=ALU.add))
        lg.free = (b_ok,)
        yield
        bv = front_banks.take()
        pe.wait(*bv.was)
        for u in range(4):
            for c in range(KC):
                t0 = g * G + u * P
                ins = nc.tensor.matmul(bv.ap[:, u * RK:(u + 1) * RK], k.hT[:, c, t0:t0 + P], wv[:, 2, c, :],
                                       start=(c == 0), stop=(c == KC - 1))
            if u < 3:
                yield
        mv = pe.inc(ins)
        vv = v_r.take()
        v_ok = a.act(vv.ap, bv.ap, ACT.Copy, mv, *vv.was)
        bv.free = (v_ok,)
        if g == NG - 1:
            slot.free = (mv,)
        made[h, g] = (q, kk, b, z, vv, q_ok, k_ok, b_ok, z_ok, v_ok)
        yield

    carried = {}
    v4 = lambda ap: ap.rearrange("p (u t) -> p u t", u=4)

    def back(h, g):
        q, kk, b, z, vv, q_ok, k_ok, b_ok, z_ok, v_ok = made.pop((h, g))
        view = lambda ap, H: ap.rearrange("p (n a i) -> p n a i", a=2, i=H)

        def factors(l):
            H = 1 << l
            d, e = d_r.take(), e_r.take()
            bv4, d4, e4 = view(b.ap, H), view(d.ap, H), view(e.ap, H)
            ref = bc(bv4[:, :, 0, H - 1], 2, H)
            d1 = pool.tt(d4[:, :, 0, :], ref, bv4[:, :, 0, :], ALU.subtract, b_ok, *d.was)
            d2 = pool.tt(d4[:, :, 1, :], bv4[:, :, 1, :], ref, ALU.subtract)
            x = a.act(d.ap, d.ap, ACT.Exp, d1, d2)
            e1 = v.tt(e4[:, :, 0, :], d4[:, :, 0, :], view(kk.ap, H)[:, :, 0, :], ALU.mult, x, k_ok, *e.was)
            e2 = v.tt(e4[:, :, 1, :], d4[:, :, 1, :], view(q.ap, H)[:, :, 1, :], ALU.mult, q_ok)
            d.free = (e2,)
            return e, e1, e2

        ahead = factors(0)
        yield
        bk, sc = back_banks.take(), st_r.take()
        pe.wait(q_ok, k_ok, *bk.was)
        for u in range(4):
            sl = slice(u * P, (u + 1) * P)
            ins = nc.tensor.matmul(bk.ap[:, sl], kk.ap[:, sl], q.ap[:, sl], start=True, stop=True)
        mm = pe.inc(ins)
        s_ok = v.tt(v4(sc.ap), v4(bk.ap), bc(k.c("ident"), 1, 4), ALU.mult, mm, *sc.was)
        bk.free = (s_ok,)
        yield
        eb, qt, kt = eb_r.take(), qt_r.take(), kt_r.take()
        for l in range(LEVELS):
            H = 1 << l
            e, e1, e2 = ahead
            if l + 1 < LEVELS:
                ahead = factors(l + 1)
                yield
            else:
                d = d_r.take()
                x1 = a.act(eb.ap, b.ap, ACT.Exp, b_ok, *eb.was)
                qt_ok = v.tt(qt.ap, q.ap, eb.ap, ALU.mult, x1, *qt.was)
                q.free = (qt_ok, mm)
                d1 = pool.tt(v4(d.ap), bc(v4(b.ap)[:, :, P - 1], 2, P), v4(b.ap), ALU.subtract, *d.was)
                b.free = (d1, x1)
                x2 = a.act(d.ap, d.ap, ACT.Exp, d1)
                d2 = v.tt(d.ap, d.ap, kk.ap, ALU.mult, x2)
                kk.free = (d2, mm)
            bk = back_banks.take()
            pe.wait(e1, e2, *bk.was)
            for u in range(4):
                sl = slice(u * P, (u + 1) * P)
                ins = nc.tensor.matmul(bk.ap[:, u * CH:(u + 1) * CH], e.ap[:, sl], view(e.ap[:, sl], H)[:, :, 1, :],
                                       start=True, stop=True)
            mm2 = pe.inc(ins)
            e.free = (mm2,)
            v.wait(mm2, s_ok)
            s_ok = v.inc(nc.vector.copy_predicated(
                out=view(sc.ap, H)[:, :, 1, :],
                mask=k.sel_queries(l),
                data=bk.ap[:, 0:G // 2].rearrange("p (n i) -> p n i", i=H)))
            bk.free = (s_ok,)
            yield
        bk = back_banks.take()
        pe.wait(d2, *bk.was)
        for u in range(4):
            sl = slice(u * P, (u + 1) * P)
            ins = nc.tensor.transpose(bk.ap[:, sl], d.ap[:, sl], k.c("ident"))
        tr = pe.inc(ins)
        d.free = (tr,)
        kt_ok = a.act(kt.ap, bk.ap, ACT.Copy, tr, *kt.was)
        bk.free = (kt_ok,)
        yield
        yield
        bs = back_banks.take()
        pe.wait(kt_ok, v_ok, *bs.was)
        for u in range(4):
            sl = slice(u * P, (u + 1) * P)
            ins = nc.tensor.matmul(bs.ap[:, sl], kt.ap[:, sl], vv.ap[:, sl], start=True, stop=True)
        ds = pe.inc(ins)
        kt.free = (ds,)
        olds = [carried.get(h)]
        for u in range(4):
            sl, old, new = slice(u * P, (u + 1) * P), olds[-1], state.take()
            if old is None:
                s_new = v.copy(new.ap, bs.ap[:, sl], ds, *new.was)
            else:
                s_new = v.stt(new.ap, old[0].ap, eb.ap[:, u * P + P - 1:u * P + P], bs.ap[:, sl], ALU.mult, ALU.add,
                              ds, x1, old[1], *new.was)
            olds.append((new, s_new))
        bs.free, eb.free = (s_new,), (s_new, qt_ok)
        yield
        bo = back_banks.take()
        pe.wait(s_ok, qt_ok, *bo.was)
        for u in range(4):
            sl, old = slice(u * P, (u + 1) * P), olds[u]
            ins = nc.tensor.matmul(bo.ap[:, sl], vv.ap[:, sl], sc.ap[:, sl], start=True, stop=old is None)
            if old is not None:
                pe.wait(old[1])
                ins = nc.tensor.matmul(bo.ap[:, sl], old[0].ap, qt.ap[:, sl], start=False, stop=True)
            mo = pe.inc(ins)
            if old is not None:
                old[0].free = (mo, olds[u + 1][1])
            if u == 1:
                yield
        carried[h] = olds[4]
        if g == NG - 1:
            carried[h][0].free = (s_new,)
        sc.free, vv.free, qt.free = (mo,), (mo,), (mo,)
        yield
        yield from norm_over_features(k, bo, mo, back_banks, sq_r, rs_r, z, z_ok, gn, g_half, h, g, 4 * EPS)

    ws = {0: load_head(0)}
    units = [(h, g) for h in range(heads) for g in range(NG)]
    for _ in front(0, 0, ws[0]):
        pass
    for i, (h, g) in enumerate(units):
        ahead = None
        if i + 1 < len(units):
            nh, ng = units[i + 1]
            if nh not in ws:
                ws[nh] = load_head(nh)
            ahead = front(nh, ng, ws[nh])
        interleave(("rec front", ahead), ("rec back", back(h, g)))


def norm_over_features(k, bo, mo, banks, sq_r, rs_r, z, z_ok, gn, g_half, block, g, eps):
    a, v, pe, nc = k.act, k.dve, k.pe, k.nc
    sq, rs = sq_r.take(), rs_r.take()
    x = a.act(sq.ap, bo.ap, ACT.Square, mo, *sq.was)
    bk = banks.take()
    pe.wait(x, *bk.was)
    mm = pe.inc(nc.tensor.matmul(bk.ap, k.c("ones"), sq.ap, start=True, stop=True))
    yield
    x = k.ln(rs.ap, bk.ap, mm, *rs.was, scale=1.0 / P, bias=k.eps_col(eps))
    bk.free = (x,)
    x = a.act(rs.ap, rs.ap, ACT.Exp, x, scale=-0.5)
    o = v.tt(sq.ap, bo.ap, rs.ap, ALU.mult, x, mm)
    bo.free, rs.free = (o,), (o,)
    o = v.stt(k.oT[:, block, g * G:(g + 1) * G], sq.ap, gn, z.ap, ALU.mult, ALU.mult, o, g_half, z_ok)
    sq.free, z.free = (o,), (o,)
    yield


def gla(k):
    psum = k.new_phase()
    fb, bb = Ring([s.ap for s in psum.slots[0:3]]), Ring([s.ap for s in psum.slots[3:8]])
    v, a, pe, pool, nc = k.dve, k.act, k.pe, k.pool, k.nc
    w_in = k.ins["w_in_2"][0]
    room = k.room
    wr = Ring([room(6 * KC * P)])
    wg = room(KC * 16).rearrange("p (c n) -> p c n", c=KC)
    low = room(T)
    up = room(256)
    bias, gn = room(2), room(1)
    got = [k.load("wg", wg, k.weights("", w_in, GLA_R, 16)),
           k.load("up", up[0:16, :], k.ins["gla_gate_up_2"][0]),
           k.vec("gb", bias, "gla_b"), k.vec("gn", gn, "gla_gn")]
    g_half = v.ts(gn, gn, 0.5, None, ALU.mult, None, got[3])
    v.wait(*got)
    a.wait(*got)
    lows = []
    for g in range(NG):
        b = fb.take()
        mm = k.project_now(b, wg, 0, g, *got, m=16)
        t = a.act(low[0:16, g * G:(g + 1) * G], b.ap[0:16, :], ACT.Copy, mm)
        b.free = (t,)
        lows.append(t)
    one = lambda n=G: Ring([room(n)])
    tmp = Ring([room(G) for _ in range(3)])
    b_r, q_r, ki_r, ks_r, eb_r = one(), one(), one(), one(), one()
    v_r, kt_r, sc_r = one(2 * G), one(), Ring([room(G) for _ in range(2)])
    z_r = Ring([room(G) for _ in range(2)])
    st = one(9 * P)
    sq_r, rs_r = one(), one()
    v4 = lambda ap: ap.rearrange("p (u t) -> p u t", u=4)
    st_prev = None
    for p in range(2):
        w = wr.take()
        wv = w.ap.rearrange("p (c n) -> p c n", c=KC)
        for c0, o, n in ((GLA_Q, 0, P), (GLA_K, P, P), (GLA_V, 2 * P, 2 * P), (GLA_Z, 4 * P, 2 * P)):
            gw = k.load("wgla", wv[:, :, o:o + n], k.weights("", w_in, c0 + p * n, n), *w.was)
        for g in range(NG):
            zs = []
            for h in range(2):
                bz, th, z = fb.take(), tmp.take(), z_r.take()
                mz = k.project_now(bz, wv, 4 * P + h * P, g, gw)
                t = k.tanh(th.ap, bz.ap, mz, *th.was, scale=0.5)
                zo = v.stt(z.ap, th.ap, 1.0, bz.ap, ALU.add, ALU.mult, t, *z.was)
                bz.free, th.free = (zo,), (zo,)
                zs.append((z, zo))
            bg = fb.take()
            pe.wait(lows[g], *bg.was)
            mg = pe.inc(nc.tensor.matmul(bg.ap, up[0:16, p * P:(p + 1) * P], low[0:16, g * G:(g + 1) * G],
                                         start=True, stop=True))
            t1, t2 = tmp.take(), tmp.take()
            read = a.act(t1.ap, bg.ap, ACT.Abs, mg, *t1.was, bias=bias[:, p:p + 1])
            x = a.act(t1.ap, t1.ap, ACT.Exp, read, scale=-1.0)
            x = k.ln(t1.ap, t1.ap, x, bias=1.0)
            y = v.ts(t2.ap, bg.ap, bias[:, p:p + 1], 0.0, ALU.add, ALU.min, mg, read, *t2.was)
            bg.free = (y,)
            y = v.tt(t2.ap, t2.ap, t1.ap, ALU.subtract, x, y)
            t1.free = (y,)
            b = b_r.take()
            v.wait(y, *b.was)
            b_ok = v.inc(nc.vector.tensor_tensor_scan(out=b.ap, data0=k.c("run64"), data1=t2.ap, initial=0.0,
                                                      op0=ALU.mult, op1=ALU.add))
            t2.free = (b_ok,)
            eb, en, es = eb_r.take(), tmp.take(), tmp.take()
            x1 = a.act(eb.ap, b.ap, ACT.Exp, b_ok, *eb.was, scale=1.0 / 16)
            x2 = a.act(en.ap, b.ap, ACT.Exp, b_ok, *en.was, scale=-1.0 / 16)
            c8 = lambda ap: ap.rearrange("p (n t) -> p n t", t=CH)
            x3 = pool.tt(c8(es.ap), bc(c8(b.ap)[:, :, CH - 1], 2, CH), c8(b.ap), ALU.subtract, b_ok, *es.was)
            x3 = a.act(es.ap, es.ap, ACT.Exp, x3, scale=1.0 / 16)
            b.free = (x1, x2, x3)
            bq = fb.take()
            mq = k.project_now(bq, wv, 0, g)
            q = q_r.take()
            q_ok = v.stt(q.ap, bq.ap, HD ** -0.5, eb.ap, ALU.mult, ALU.mult, mq, x1, *q.was)
            bq.free = (q_ok,)
            bk = fb.take()
            mk = k.project_now(bk, wv, P, g)
            ki, ks = ki_r.take(), ks_r.take()
            ki_ok = v.tt(ki.ap, bk.ap, en.ap, ALU.mult, mk, x2, *ki.was)
            ks_ok = v.tt(ks.ap, bk.ap, es.ap, ALU.mult, mk, x3, *ks.was)
            bk.free, en.free, es.free = (ks_ok,), (ki_ok,), (ks_ok,)
            vv = v_r.take()
            vvv = vv.ap.rearrange("p (u n) -> p u n", u=4)
            for half in range(2):
                b2 = fb.take()
                pe.wait(*b2.was)
                for u in range(2):
                    t0 = g * G + (2 * half + u) * P
                    for c in range(KC):
                        ins = nc.tensor.matmul(b2.ap[:, u * 256:(u + 1) * 256], k.hT[:, c, t0:t0 + P],
                                               wv[:, c, 2 * P:4 * P], start=(c == 0), stop=(c == KC - 1))
                mm = pe.inc(ins)
                v_ok = a.act(vvv[:, 2 * half:2 * half + 2, :], b2.ap.rearrange("p (u n) -> p u n", u=2), ACT.Copy,
                             mm, *vv.was)
                b2.free = (v_ok,)
            if g == NG - 1:
                w.free = (mm,)
            b2, kt = bb.take(), kt_r.take()
            pe.wait(ks_ok, *b2.was)
            for u in range(4):
                ins = nc.tensor.transpose(b2.ap[:, u * P:(u + 1) * P], ks.ap[:, u * P:(u + 1) * P], k.c("ident"))
            tr = pe.inc(ins)
            ks.free = (tr,)
            kt_ok = a.act(kt.ap, b2.ap, ACT.Copy, tr, *kt.was)
            b2.free = (kt_ok,)
            scs, b2 = [], [bb.take(), bb.take()]
            pe.wait(q_ok, ki_ok, *b2[0].was, *b2[1].was)
            for u in range(4):
                for h in range(2):
                    rows, sl = slice(64 * h, 64 * h + 64), slice(u * P, (u + 1) * P)
                    ins = nc.tensor.matmul(b2[h].ap[:, sl], ki.ap[rows, sl], q.ap[rows, sl], start=True, stop=True)
            mm = pe.inc(ins)
            ki.free = (mm,)
            for h in range(2):
                sc = sc_r.take()
                s_ok = v.tt(v4(sc.ap), v4(b2[h].ap), bc(k.c("gla"), 1, 4), ALU.mult, mm, *sc.was)
                b2[h].free = (s_ok,)
                scs.append((sc, s_ok))
            b2 = [bb.take(), bb.take()]
            pe.wait(kt_ok, v_ok, *b2[0].was, *b2[1].was)
            kt3 = v4(kt.ap)
            for u in range(4):
                for c in range(2):
                    for h in range(2):
                        rows = slice(64 * c, 64 * c + 64)
                        ins = nc.tensor.matmul(b2[c].ap[64 * h:64 * h + 64, u * P:(u + 1) * P],
                                               kt3[rows, u, 64 * h:64 * h + 64], vvv[rows, u, h * P:(h + 1) * P],
                                               start=True, stop=True)
            mm = pe.inc(ins)
            kt.free = (mm,)
            s = st.take()
            s3 = s.ap.rearrange("p (i n) -> p i n", n=P)
            if g == 0:
                v.wait(*s.was)
                last = v.inc(nc.vector.memset(s3[:, 0, :], 0.0))
            else:
                last = v.copy(s3[:, 0, :], s3[:, 8, :], *s.was)
            for i in range(8):
                last = v.stt(s3[:, i + 1, :], s3[:, i, :], eb.ap[:, i * CH + CH - 1:(i + 1) * CH],
                             b2[i % 2].ap[:, (i // 2) * P:(i // 2 + 1) * P], ALU.mult, ALU.add, last, mm)
            b2[0].free = b2[1].free = (last,)
            eb.free = (last, q_ok)
            outs = [bb.take(), bb.take()]
            pe.wait(last, *outs[0].was, *outs[1].was)
            for h in range(2):
                sc, s_ok = scs[h]
                pe.wait(s_ok)
                rows = slice(64 * h, 64 * h + 64)
                for u in range(4):
                    sl = slice(u * P, (u + 1) * P)
                    nc.tensor.matmul(outs[h].ap[:, sl], vvv[:, u, h * P:(h + 1) * P], sc.ap[:, sl],
                                     start=True, stop=False)
                    for c in range(2):
                        t0 = u * P + c * CH
                        ins = nc.tensor.matmul(outs[h].ap[:, t0:t0 + CH], s3[rows, 2 * u + c, :],
                                               q.ap[rows, t0:t0 + CH], start=False, stop=(c == 1))
                mo = pe.inc(ins)
                sc.free = (mo,)
                z, zo = zs[h]
                for _ in norm_over_features(k, outs[h], mo, bb, sq_r, rs_r, z, zo, gn, g_half, 2 * p + h, g, EPS):
                    pass
            vv.free, s.free, q.free = (mo,), (mo,), (mo,)


GD = 256
ND = T // GD
UD = GD // P
CD = GD // CH


def delta_rule(k):
    psum = k.new_phase()
    fb, bb = Ring([s.ap for s in psum.slots[0:3]]), Ring([s.ap for s in psum.slots[3:8]])
    v, a, pe, pool, nc = k.dve, k.act, k.pe, k.pool, k.nc
    w_in = k.ins["w_in_2"][0]
    room = k.room
    wr = Ring([room(4 * KC * P)])
    wa = room(T)
    up = room(512)
    cols = room(64)
    o0, off = COLUMNS["rwkv"]
    names = {n: COLUMNS[n][0] - o0 for n in ("mu", "w0", "a0", "kk", "ka", "rk", "lw", "lb")}
    tok = [k.vec("rwkv", cols[:, 0:off], "rwkv")]
    names["nm"] = off
    col = lambda name, i: cols[:, names[name] + i:names[name] + i + 1]
    tok.append(v.ts(cols[:, off:off + 13], cols[:, 0:13], -1.0, 1.0, ALU.mult, ALU.add, *tok))
    tok.append(v.ts(cols[:, names["w0"]:names["w0"] + 8], cols[:, names["w0"]:names["w0"] + 8], 0.5, None, ALU.mult,
                    None, *tok))
    tok.append(k.load("up", up[0:64, :], k.ins["rwkv_w_up_2"][0]))
    tok.append(k.load("up2", up[64:128, :], k.ins["rwkv_a_up_2"][0]))
    ring = lambda n, w=GD: Ring([room(w) for _ in range(n)])
    shift = {n: ring(1, GD + 1) for n in "rkvw"}

    def mixed(kind, bank, mm, j, g, out, *w):
        s = shift[kind].take()
        if g == 0:
            x = a.act(s.ap[:, 0:1], cols[:, 0:1], ACT.Copy, *s.was, *tok, scale=0.0)
        else:
            x = a.act(s.ap[:, 0:1], s.ap[:, GD:GD + 1], ACT.Copy, *s.was)
        y = a.act(s.ap[:, 1:GD + 1], bank.ap[:, 0:GD], ACT.Identity, mm, x, scale=col("mu", j))
        z = v.stt(out, bank.ap[:, 0:GD], col("nm", j), s.ap[:, 0:GD], ALU.mult, ALU.add, y, x, *tok, *w)
        s.free = (z,)
        return z

    w = wr.take()
    wv = w.ap.rearrange("p (i c n) -> p i c n", i=4, c=KC)
    gw = k.load("wd", wv[:, 0], k.weights("", w_in, RW_WA, P))
    was = []
    for g in range(ND):
        b = fb.take()
        mm = k.project_now(b, wv[:, 0], 0, g, gw, width=GD)
        sl = slice(g * GD, (g + 1) * GD)
        t = mixed("w", b, mm, 12, g, wa[:, sl])
        b.free = (t,)
        t2 = a.act(wa[0:64, sl], wa[0:64, sl], ACT.Tanh, t)
        was.append((t, t2))
    w.free = (mm,)
    hand = {n: ring(2) for n in ("v", "z", "beta", "kappa", "bon", "eb")}
    ar_r = ring(2, 2 * GD)
    own = {n: ring(1) for n in ("r", "k", "gl", "b", "av", "kk", "kp")}
    tmp = ring(4)
    tm = {n: ring(1) for n in ("beta", "kappa", "v")}
    rhs_r, wu_r, xz_r = ring(1, 2 * GD), ring(1, 2 * GD), ring(1, 2 * GD)
    m_r = ring(1, 4 * GD)
    t1_r, gt_r, bu_r, y_r, sq_r = ring(1), ring(1), ring(1), ring(1), ring(1)
    st_r = ring(1, (CD + 1) * CH)
    c_ln = float(np.exp(-0.5)) / 2
    made = {}

    def load_pair(p):
        w = wr.take()
        wv = w.ap.rearrange("p (i c n) -> p i c n", i=4, c=KC)
        for i, c0 in enumerate((RW_R, RW_K, RW_V, RW_Z)):
            gw = k.load("wd", wv[:, i], k.weights("", w_in, c0 + p * P, P), *w.was)
        return w, wv, gw

    def front(p, g, pair):
        w, wv, gw = pair
        cs = slice(g * GD, (g + 1) * GD)
        r, kf = own["r"].take(), own["k"].take()
        vf, z = hand["v"].take(), hand["z"].take()
        oks = []
        for i, (kind, dst) in enumerate((("r", r), ("k", kf), ("v", vf))):
            b = fb.take()
            mm = yield from k.project(b, wv[:, i], 0, g, gw, width=GD)
            ok = mixed(kind, b, mm, 4 * i + p, g, dst.ap, *dst.was)
            b.free = (ok,)
            oks.append(ok)
            yield
        r_ok, k_ok, v_ok = oks
        b = fb.take()
        mm = yield from k.project(b, wv[:, 3], 0, g, width=GD)
        if g == ND - 1:
            w.free = (mm,)
        th = tmp.take()
        x = k.tanh(th.ap, b.ap[:, 0:GD], mm, *th.was, scale=0.5)
        z_ok = v.stt(z.ap, th.ap, 1.0, b.ap[:, 0:GD], ALU.add, ALU.mult, x, *z.was)
        b.free, th.free = (z_ok,), (z_ok,)
        ths = []
        for i, name in enumerate(("w0", "a0")):
            b, th = fb.take(), tmp.take()
            rows = slice(64 * i, 64 * i + 64)
            pe.wait(*was[g], *tok, *b.was)
            mm = pe.inc(nc.tensor.matmul(b.ap[:, 0:GD], up[rows, p * P:(p + 1) * P], wa[rows, cs],
                                         start=True, stop=True))
            x = k.tanh(th.ap, b.ap[:, 0:GD], mm, *th.was, scale=0.5, bias=col(name, p))
            b.free = (x,)
            ths.append((th, x))
        gl, bcum, av = own["gl"].take(), own["b"].take(), own["av"].take()
        gl_ok = v.ts(gl.ap, ths[0][0].ap, -c_ln, -c_ln, ALU.mult, ALU.add, ths[0][1], *gl.was)
        av_ok = v.ts(av.ap, ths[1][0].ap, 0.5, 0.5, ALU.mult, ALU.add, ths[1][1], *av.was)
        ths[0][0].free, ths[1][0].free = (gl_ok,), (av_ok,)
        v.wait(gl_ok, *bcum.was)
        b_ok = v.inc(nc.vector.tensor_tensor_scan(out=bcum.ap, data0=k.c("run64")[:, 0:GD], data1=gl.ap, initial=0.0,
                                                  op0=ALU.mult, op1=ALU.add))
        yield
        kk = own["kk"].take()
        kk0 = v.ts(kk.ap, kf.ap, col("kk", p), None, ALU.mult, None, k_ok, *kk.was)
        sq = tmp.take()
        x = a.act(sq.ap, kk.ap, ACT.Square, kk0, *sq.was)
        b = fb.take()
        pe.wait(x, *b.was)
        mm = pe.inc(nc.tensor.matmul(b.ap[:, 0:GD], k.c("head_ones"), sq.ap, start=True, stop=True))
        x = v.ts(sq.ap, b.ap[:, 0:GD], 1e-24, 2.0 ** 18, ALU.max, ALU.mult, mm)
        b.free = (x,)
        x = k.ln(sq.ap, sq.ap, x)
        x = a.act(sq.ap, sq.ap, ACT.Exp, x, scale=-0.5, bias=k.eps_col(NINE_LN2))
        kk_ok = v.tt(kk.ap, kk.ap, sq.ap, ALU.mult, x, kk0)
        sq.free = (kk_ok,)
        kp, t = own["kp"].take(), tmp.take()
        x = v.ts(t.ap, av.ap, -1.0, col("ka", p), ALU.add, ALU.mult, av_ok, *t.was)
        kp_ok = v.stt(kp.ap, t.ap, 1.0, kf.ap, ALU.add, ALU.mult, x, k_ok, *kp.was)
        t.free, kf.free = (kp_ok,), (kp_ok,)
        yield
        bn, t = hand["bon"].take(), tmp.take()
        x = v.stt(t.ap, r.ap, col("rk", p), kp.ap, ALU.mult, ALU.mult, r_ok, kp_ok, *t.was)
        b = fb.take()
        pe.wait(x, *b.was)
        mm = pe.inc(nc.tensor.matmul(b.ap[:, 0:GD], k.c("head_ones"), t.ap, start=True, stop=True))
        t.free = (mm,)
        bn_ok = v.tt(bn.ap, b.ap[:, 0:GD], vf.ap, ALU.mult, mm, v_ok, *bn.was)
        b.free = (bn_ok,)
        ar, beta, kappa, eb = ar_r.take(), hand["beta"].take(), hand["kappa"].take(), hand["eb"].take()
        ar3 = ar.ap.rearrange("p (m t) -> p m t", m=2)
        t = tmp.take()
        x = pool.tt(t.ap, bcum.ap, gl.ap, ALU.subtract, b_ok, gl_ok, *t.was)
        gl.free = (x, b_ok)
        x = a.act(t.ap, t.ap, ACT.Exp, x)
        al_ok = v.stt(ar3[:, 0, :], kk.ap, -1.0, t.ap, ALU.mult, ALU.mult, x, kk_ok, *ar.was)
        t.free = (al_ok,)
        e_ok = a.act(eb.ap, bcum.ap, ACT.Exp, b_ok, *eb.was)
        rho_ok = v.tt(ar3[:, 1, :], r.ap, eb.ap, ALU.mult, e_ok, r_ok)
        r.free = (rho_ok,)
        t = tmp.take()
        x = a.act(t.ap, bcum.ap, ACT.Exp, b_ok, *t.was, scale=-1.0)
        bcum.free = (x,)
        y = pool.tt(beta.ap, kk.ap, av.ap, ALU.mult, kk_ok, av_ok, *beta.was)
        kk.free, av.free = (y, al_ok), (y,)
        be_ok = v.tt(beta.ap, beta.ap, t.ap, ALU.mult, x, y)
        ka_ok = v.tt(kappa.ap, kp.ap, t.ap, ALU.mult, x, kp_ok, *kappa.was)
        kp.free, t.free = (ka_ok,), (ka_ok, be_ok)
        made[p, g] = dict(ar=ar, ar3=ar3, beta=beta, kappa=kappa, eb=eb, vf=vf, z=z, bn=bn, al_ok=al_ok,
                          rho_ok=rho_ok, be_ok=be_ok, ka_ok=ka_ok, e_ok=e_ok, v_ok=v_ok, z_ok=z_ok, bn_ok=bn_ok)
        yield

    tiles = [(u, c, h) for u in range(UD) for c in range(2) for h in range(2)]
    half = lambda i: slice(64 * i, 64 * i + 64)
    by_uh = lambda ap: ap.rearrange("p (u h n) -> p u h n", u=UD, h=2)
    by_u = lambda ap: ap.rearrange("p (u n) -> p u n", u=UD)
    at = lambda u, h, n: slice((2 * u + h) * n, (2 * u + h + 1) * n)

    def back(p, g):
        f = made.pop((p, g))
        ar3, beta, kappa, eb = f["ar3"], f["beta"], f["kappa"], f["eb"]
        cs = slice(g * GD, (g + 1) * GD)
        rh = rhs_r.take()
        rh4 = by_uh(rh.ap)
        tms = {}
        for name, src, ok in (("alpha", ar3[:, 0, :], f["al_ok"]), ("beta", beta.ap, f["be_ok"]),
                              ("kappa", kappa.ap, f["ka_ok"]), ("v", f["vf"].ap, f["v_ok"])):
            b1 = bb.take()
            pe.wait(ok, *b1.was)
            for u in range(UD):
                ins = nc.tensor.transpose(b1.ap[:, u * P:(u + 1) * P], src[:, u * P:(u + 1) * P], k.c("ident"))
            tr = pe.inc(ins)
            if name == "alpha":
                o = a.act(rh4[:, :, :, 0:64], by_uh(b1.ap[:, 0:GD]), ACT.Copy, tr, *rh.was)
                a_tm = o
            else:
                dst = tm[name].take()
                o = a.act(dst.ap, b1.ap[:, 0:GD], ACT.Copy, tr, *dst.was)
                tms[name] = (dst, by_u(dst.ap), o)
            b1.free = (o,)
        f["vf"].free = (tr, f["bn_ok"])
        yield
        m = m_r.take()
        m4 = by_uh(m.ap)
        b2 = [bb.take(), bb.take()]
        pe.wait(f["al_ok"], f["rho_ok"], f["be_ok"], f["ka_ok"], *b2[0].was, *b2[1].was)
        for u, c, h in tiles:
            t0 = u * P + c * CH
            for i, src in enumerate((beta, kappa)):
                o0 = u * 256 + i * 128
                ins = nc.tensor.matmul(b2[h].ap[half(c), o0:o0 + 128], src.ap[half(h), t0:t0 + CH],
                                       ar3[half(h), :, t0:t0 + CH], start=True, stop=True)
        mm = pe.inc(ins)
        for h in range(2):
            m_ok = v.tt(m4[:, :, h, :], by_u(b2[h].ap), bc(k.c("delta"), 1, UD), ALU.mult, mm, *m.was)
            b2[h].free = (m_ok,)
        b2 = [bb.take(), bb.take()]
        pe.wait(*b2[0].was, *b2[1].was)
        for u, c, h in tiles:
            t0 = u * P + c * CH
            ins = nc.tensor.matmul(b2[h].ap[half(c), u * CH:(u + 1) * CH], ar3[half(h), 0, t0:t0 + CH],
                                   beta.ap[half(h), t0:t0 + CH], start=True, stop=True)
        mm = pe.inc(ins)
        beta.free, kappa.free = (mm,), (mm,)
        xz = xz_r.take()
        xz5 = xz.ap.rearrange("p (u h m n) -> p u h m n", u=UD, h=2, m=2)
        for h in range(2):
            x1 = v.tt(xz5[:, :, h, 0, :], by_u(b2[h].ap[:, 0:UD * CH]), bc(k.c("low0"), 1, UD), ALU.mult, mm, *xz.was)
            b2[h].free = (x1,)
            x2 = v.tt(xz5[:, :, h, 1, :], m4[:, :, h, 0:64], bc(k.c("up0"), 1, UD), ALU.mult, m_ok)
        xzf = xz.ap.rearrange("p (n j) -> p n j", j=CH)
        x_ok = v.tt(xzf, xzf, bc(k.c("eye64"), 1, 4 * UD), ALU.add, x1, x2)
        yield
        for l in range(1, 6):
            b1, t1 = bb.take(), t1_r.take()
            pe.wait(x_ok, m_ok, *b1.was)
            for u, c, h in tiles:
                ins = nc.tensor.matmul(b1.ap[half(c), at(u, h, CH)], m4[half(c), u, h, 0:64], xz5[half(c), u, h, 0, :],
                                       start=True, stop=True)
            mm = pe.inc(ins)
            t_ok = v.tt(t1.ap.rearrange("p (n j) -> p n j", j=CH), b1.ap[:, 0:GD].rearrange("p (n j) -> p n j", j=CH),
                        bc(k.c(f"low{l}"), 1, 2 * UD), ALU.mult, mm, *t1.was)
            b1.free = (t_ok,)
            yield
            t14 = by_uh(t1.ap)
            b1 = bb.take()
            pe.wait(t_ok, *b1.was)
            for u, c, h in tiles:
                o0 = (2 * u + h) * P
                nc.tensor.matmul(b1.ap[half(c), o0:o0 + CH], xz5[half(c), u, h, 1, :], t14[half(c), u, h, :],
                                 start=True, stop=True)
                ins = nc.tensor.matmul(b1.ap[half(c), o0 + CH:o0 + P], t14[half(c), u, h, :], xz5[half(c), u, h, 1, :],
                                       start=True, stop=True)
            mm = pe.inc(ins)
            t1.free = (mm,)
            x_ok = v.tt(xz.ap, xz.ap, b1.ap, ALU.add, mm)
            b1.free = (x_ok,)
            yield
        (vt, vt3, vt_ok), (bt, bt3, bt_ok), (kt, kt3, kt_ok) = tms["v"], tms["beta"], tms["kappa"]
        b1 = bb.take()
        pe.wait(m_ok, vt_ok, *b1.was)
        for u, c, h in tiles:
            ins = nc.tensor.matmul(b1.ap[half(c), at(u, h, CH)], m4[half(c), u, h, 128:192], vt3[half(c), u, half(h)],
                                   start=True, stop=True)
        mm = pe.inc(ins)
        o = a.act(rh4[:, :, :, 64:128], by_uh(b1.ap[:, 0:GD]), ACT.Copy, mm)
        b1.free = (o,)
        yield
        wu = wu_r.take()
        wu4 = by_uh(wu.ap)
        b1 = bb.take()
        pe.wait(o, a_tm, x_ok, *b1.was)
        for u, c, h in tiles:
            ins = nc.tensor.matmul(b1.ap[half(c), at(u, h, P)], xz5[half(c), u, h, 1, :], rh4[half(c), u, h, :],
                                   start=True, stop=True)
        mm = pe.inc(ins)
        xz.free, rh.free = (mm, x_ok), (mm,)
        w_ok = a.act(wu.ap, b1.ap, ACT.Copy, mm, *wu.was)
        b1.free = (w_ok,)
        yield
        b2 = [bb.take(), bb.take()]
        pe.wait(w_ok, bt_ok, kt_ok, *b2[0].was, *b2[1].was)
        for u, c, h in tiles:
            bk, n0 = b2[c].ap, u * P
            nc.tensor.matmul(bk[half(h), n0:n0 + CH], wu4[half(c), u, h, 0:64], bt3[half(c), u, half(h)],
                             start=True, stop=True)
            nc.tensor.matmul(bk[half(h), n0 + CH:n0 + P], bt3[half(c), u, half(h)], wu4[half(c), u, h, 64:128],
                             start=True, stop=False)
            ins = nc.tensor.matmul(bk[half(h), n0 + CH:n0 + P], kt3[half(c), u, half(h)], vt3[half(c), u, half(h)],
                                   start=False, stop=True)
        mm = pe.inc(ins)
        bt.free, kt.free = (mm,), (mm,)
        gt, bu, s = gt_r.take(), bu_r.take(), st_r.take()
        by_uc = lambda ap: ap.rearrange("p (u c n) -> p u c n", u=UD, c=2)
        gt4, bu4, eb4 = by_uc(gt.ap), by_uc(bu.ap), by_uc(eb.ap)
        for c in range(2):
            b4 = b2[c].ap[:, 0:UD * P].rearrange("p (u m n) -> p u m n", u=UD, m=2)
            g_ok = v.tt(gt4[:, :, c, :], b4[:, :, 0, :], bc(k.c("eye64"), 1, UD), ALU.add, mm, *gt.was)
            u_ok = v.tt(bu4[:, :, c, :], b4[:, :, 1, :], bc(eb4[:, :, c, CH - 1], 2, CH), ALU.mult, f["e_ok"], *bu.was)
            b2[c].free = (u_ok, g_ok)
        b2 = [bb.take(), bb.take()]
        pe.wait(*b2[0].was, *b2[1].was)
        for u, c, h in tiles:
            ins = nc.tensor.matmul(b2[c].ap[half(h), u * CH:(u + 1) * CH], wu4[half(c), u, h, 0:64],
                                   m4[half(c), u, h, 64:128], start=True, stop=True)
        mm = pe.inc(ins)
        rho = by_uc(ar3[:, 1, :])
        for c in range(2):
            rho2 = v.tt(rho[:, :, c, :], rho[:, :, c, :], by_u(b2[c].ap[:, 0:UD * CH]), ALU.add, mm)
            b2[c].free = (rho2,)
        yield
        s3 = s.ap.rearrange("p (i n) -> p i n", n=CH)
        if g == 0:
            v.wait(*s.was)
            s_ok = v.inc(nc.vector.memset(s3[:, 0, :], 0.0))
        else:
            s_ok = v.copy(s3[:, 0, :], s3[:, CD, :], *s.was)
        for i in range(CD):
            b1 = bb.take()
            pe.wait(s_ok, g_ok, *b1.was)
            for h in range(2):
                ins = nc.tensor.matmul(b1.ap[half(h), 0:CH], gt4[half(h), i // 2, i % 2, :], s3[half(h), i, :],
                                       start=True, stop=True)
            mm = pe.inc(ins)
            s_ok = v.stt(s3[:, i + 1, :], b1.ap[:, 0:CH], eb.ap[:, i * CH + CH - 1:(i + 1) * CH],
                         bu4[:, i // 2, i % 2, :], ALU.mult, ALU.add, mm, u_ok)
            b1.free = (s_ok,)
            yield
        gt.free, bu.free, eb.free = (mm,), (s_ok,), (s_ok, f["rho_ok"])
        b2, b1 = [bb.take(), bb.take()], bb.take()
        pe.wait(s_ok, rho2, *b2[0].was, *b2[1].was, *b1.was)
        for u, c, h in tiles:
            out = b2[c].ap[half(h), u * CH:(u + 1) * CH]
            nc.tensor.matmul(out, wu4[half(c), u, h, 64:128], m4[half(c), u, h, 64:128], start=True, stop=False)
            nc.tensor.matmul(out, vt3[half(c), u, half(h)], m4[half(c), u, h, 192:256], start=False, stop=True)
        for u, c, h in tiles:
            t0 = u * P + c * CH
            ins = nc.tensor.matmul(b1.ap[half(h), t0:t0 + CH], s3[half(h), 2 * u + c, :], ar3[half(h), 1, t0:t0 + CH],
                                   start=True, stop=True)
        mm = pe.inc(ins)
        wu.free, m.free, vt.free, s.free, f["ar"].free = (mm,), (mm, x2), (mm,), (mm, s_ok), (mm, tr, rho2)
        y = y_r.take()
        y_ok = a.act(y.ap, b1.ap[:, 0:GD], ACT.Copy, mm, *y.was)
        b1.free = (y_ok,)
        for c in range(2):
            y4 = by_uc(y.ap)[:, :, c, :]
            y_ok2 = v.tt(y4, y4, by_u(b2[c].ap[:, 0:UD * CH]), ALU.add, mm, y_ok)
            b2[c].free = (y_ok2,)
        y_ok = y_ok2
        yield
        b1 = bb.take()
        pe.wait(y_ok, *b1.was)
        mm = pe.inc(nc.tensor.matmul(b1.ap[:, 0:GD], k.c("head_ones"), y.ap, start=True, stop=True))
        x = v.stt(y.ap, b1.ap[:, 0:GD], -1.0 / HD, y.ap, ALU.mult, ALU.add, mm)
        b1.free = (x,)
        sq = sq_r.take()
        x2 = a.act(sq.ap, y.ap, ACT.Square, x, *sq.was)
        b1 = bb.take()
        pe.wait(x2, *b1.was)
        mm = pe.inc(nc.tensor.matmul(b1.ap[:, 0:GD], k.c("head_ones"), sq.ap, start=True, stop=True))
        x2 = a.act(sq.ap, b1.ap[:, 0:GD], ACT.Ln, mm, scale=1.0 / HD, bias=k.eps_col(GN_EPS))
        b1.free = (x2,)
        x2 = a.act(sq.ap, sq.ap, ACT.Exp, x2, scale=-0.5)
        x = v.tt(y.ap, y.ap, sq.ap, ALU.mult, x, x2)
        sq.free = (x,)
        x = v.ts(y.ap, y.ap, col("lw", p), col("lb", p), ALU.mult, ALU.add, x)
        x = v.tt(y.ap, y.ap, f["bn"].ap, ALU.add, x, f["bn_ok"])
        f["bn"].free = (x,)
        x = v.stt(k.oT[:, 4 + p, cs], y.ap, 0.5, f["z"].ap, ALU.mult, ALU.mult, x, f["z_ok"])
        y.free, f["z"].free = (x,), (x,)
        yield

    groups = [(p, g) for p in range(4) for g in range(ND)]
    pairs = {0: load_pair(0)}
    for _ in front(0, 0, pairs[0]):
        pass
    for i, (p, g) in enumerate(groups):
        ahead = None
        if i + 1 < len(groups):
            np_, ng = groups[i + 1]
            if np_ not in pairs:
                pairs[np_] = load_pair(np_)
            ahead = front(np_, ng, pairs[np_])
        interleave(("delta front", ahead), ("delta back", back(p, g)))


def build(nc, ins, out, x1, x2, table, select, at):
    with ExitStack() as ctx:
        k = Core(nc, ctx, ins, at)
        k.load_constants(table, select)
        x0 = ins["x"][0]
        first_norm(k)
        attention(k)
        attention_gate(k)
        finish_layer(k, 0, x0, x1, ins["attn_w_out"][0], ins["attn_b_out"][0], ins["post_norm_w"][0],
                     "pre1", None)
        recurrence(k)
        finish_layer(k, 1, x1, x2, ins["rec_w_out"][0], None, ins["post_norm_w"][1], "norm2", None)
        gla(k)
        delta_rule(k)
        finish_layer(k, 2, x2, out, ins["w_out_2"][0], None, None, None, ins["final_norm_w_2"])
        k.sp.wait(*k.dma.stores)


_INS = ["x", "pre_norm_w", "post_norm_w", "attn_w_in", "attn_b_in", "attn_sinks", "attn_w_out",
        "attn_b_out", "rec_w_in", "rec_lb_logits", "rec_gnorm_w", "rec_w_out", "norm_w_2", "w_in_2",
        "gla_gate_up_2", "gla_gate_bias_2", "gla_norm_w_2", "rwkv_mu_2", "rwkv_w0_2", "rwkv_w_up_2", "rwkv_a0_2",
        "rwkv_a_up_2", "rwkv_k_k_2", "rwkv_k_a_2", "rwkv_r_k_2", "rwkv_ln_w_2", "rwkv_ln_b_2", "w_out_2",
        "final_norm_w_2"]


def kernel(**inputs):
    import concourse.bacc as _bacc
    from concourse.bass_utils import run_bass_kernel_spmd as _run

    nc = _bacc.Bacc("TRN2", target_bir_lowering=False, num_devices=1, dynamic_dma_scratch_size=1024)
    table, at, select = constant_tables()
    arrays, ins = {}, {}
    for name in _INS:
        a = np.ascontiguousarray(inputs[name])
        arrays[f"in_{name}"] = a
        ins[name] = nc.dram_tensor(f"in_{name}", a.shape, mybir.dt.from_np(a.dtype), kind="ExternalInput").ap()
    positions = np.ascontiguousarray(np.asarray(inputs["positions"]).reshape(NT, P).T)
    for name, a in (("table", table), ("select", select), ("columns", feature_columns(inputs)),
                    ("positions", positions)):
        arrays[name] = a
        ins[name] = nc.dram_tensor(name, a.shape, mybir.dt.from_np(a.dtype), kind="ExternalInput").ap()
    out = nc.dram_tensor("out", (1, T, D), F32, kind="ExternalOutput").ap()
    x1 = nc.dram_tensor("x_after_0", (T, D), F32, kind="Internal").ap()
    x2 = nc.dram_tensor("x_after_1", (T, D), F32, kind="Internal").ap()
    build(nc, ins, out[0], x1, x2, ins["table"], ins["select"], at)
    r = _run(nc, [arrays], core_ids=[0])
    return r.results[0]["out"]
```

```python
from contextlib import ExitStack

import numpy as np
import concourse.bass as bass
from concourse import mybir

F32 = mybir.dt.float32
F32R = mybir.dt.float32r
I32 = mybir.dt.int32
I8 = mybir.dt.int8
ACT = mybir.ActivationFunctionType
ALU = mybir.AluOpType
AX = mybir.AxisListType

P = 128
T = 2048
D = 1024
NT = T // P
KC = D // P
G = 512
NG = T // G
EPS = 1e-6
HD = 64
NH = 16
NKV = 2
GRP = NH // NKV
QUAD = 4
ROPE = HD // 4
RH = ROPE // 2
KV0 = NH * HD
V0 = KV0 + NKV * HD
Z0 = V0 + NKV * HD
QKV = Z0
RK = 128
LEVELS = 7
CH = 64
GLA_Q, GLA_K, GLA_V, GLA_R, GLA_Z = 0, 256, 512, 1024, 1040
RW = 1552
RW_R, RW_K, RW_V, RW_WA, RW_Z = RW, RW + 512, RW + 1024, RW + 1536, RW + 1664
GD = 128
ND = T // GD
GN_EPS = 64e-5
NEG = -1e30
NINE_LN2 = 9 * float(np.log(2.0))


VECTORS = {
    "pre0": ("pre_norm_w", 0, 8), "pre1": ("pre_norm_w", 1, 8), "norm2": ("norm_w_2", 0, 8),
    "att_b": ("attn_b_in", 0, 18), "lb0": ("rec_lb_logits", 0, 8), "lb1": ("rec_lb_logits", 1, 8),
    "rec_gn": ("rec_gnorm_w", 0, 1), "gla_b": ("gla_gate_bias_2", 0, 2), "gla_gn": ("gla_norm_w_2", 0, 1),
    "mu": ("rwkv_mu_2", 0, 13), "w0": ("rwkv_w0_2", 0, 4), "a0": ("rwkv_a0_2", 0, 4),
    "kk": ("rwkv_k_k_2", 0, 4), "ka": ("rwkv_k_a_2", 0, 4), "rk": ("rwkv_r_k_2", 0, 4),
    "lw": ("rwkv_ln_w_2", 0, 4), "lb": ("rwkv_ln_b_2", 0, 4),
}
COLUMNS, _at = {}, 0
for _name, (_, _, _n) in VECTORS.items():
    COLUMNS[_name] = (_at, _n)
    _at += _n
COLUMNS["att_zb"] = (COLUMNS["att_b"][0] + Z0 // P, D // P)
COLUMNS["rwkv"] = (COLUMNS["mu"][0], _at - COLUMNS["mu"][0])


def feature_columns(inputs):
    return np.ascontiguousarray(np.concatenate(
        [np.asarray(inputs[src])[row].reshape(-1, P).T for src, row, _ in VECTORS.values()], 1))


def constant_tables():
    s = np.arange(P)[:, None]
    t = np.arange(P)[None, :]
    chunk = s // CH == t // CH
    col = np.arange(G)[None, :] + 0 * s
    inv = np.float32(500000.0) ** (-(np.arange(RH, dtype=np.float32) * np.float32(2.0) / np.float32(ROPE)))
    delta = {"strict_incl": np.concatenate([chunk & (s < t), chunk & (s <= t)], 1)}
    for l in range(6):
        h = 1 << l
        delta[f"low{l}"] = (s // (2 * h) == t // (2 * h)) & (s % (2 * h) >= h) & (t % (2 * h) < h)
    delta["up0"] = (s // 2 == t // 2) & (s < t)
    delta["eye64"] = (s % CH == np.arange(CH)[None, :])
    delta["run64"] = (col % CH != 0)[:, 0:GD]
    phases = {
        "common": {"ident": (s == t), "head_ones": (s // HD == t // HD), "ones": np.ones((P, P))},
        "attention": {"band": np.concatenate([np.where(t > s, 0.0, NEG), np.where(t <= s, 0.0, NEG)], 1),
                      "freq": np.tile(inv.astype(np.float32)[None, :], (P, NT))},
        "recurrence": {"run128": (col % P != 0)},
        "gla": {"run64": (col % CH != 0), "mask": chunk & (s <= t)},
        "delta": delta,
    }
    cols, spans, at, off = [], {}, {}, 0
    for phase, parts in phases.items():
        start, at[phase] = off, {}
        for name, a in parts.items():
            a = np.ascontiguousarray(a, dtype=np.float32)
            at[phase][name] = (off - start, a.shape[1])
            off += a.shape[1]
            cols.append(a)
        spans[phase] = (start, off - start)
    masks = []
    for l in range(LEVELS):
        h = 1 << l
        m = (s // (2 * h) == t // (2 * h)) & (s % (2 * h) < h)
        masks += [m[:, (np.arange(P) % (2 * h)) >= h]] * (G // P)
    select = np.concatenate(masks, 1).astype(np.float32)
    return np.concatenate(cols, 1), spans, at, select


def bc(ap, axis, n):
    a = ap.unsqueeze(axis)
    shape = list(a.shape)
    shape[axis] = n
    return a.broadcast_to(shape)


class Engine:

    def __init__(self, eng, sem):
        self.e, self.sem, self.n, self.seen = eng, sem, 0, {}

    def wait(self, *tokens):
        for sem, value in tokens:
            if self.seen.get(sem.num, 0) < value:
                self.seen[sem.num] = value
                self.e.wait_ge(sem, value)

    def inc(self, ins):
        self.n += 1
        ins.then_inc(self.sem, 1)
        return (self.sem, self.n)

    def tt(self, out, a, b, op, *w):
        self.wait(*w)
        return self.inc(self.e.tensor_tensor(out, a, b, op))

    def ts(self, out, a, s1, s2, op0, op1, *w):
        self.wait(*w)
        if s2 is None:
            return self.inc(self.e.tensor_scalar(out, a, s1, None, op0))
        return self.inc(self.e.tensor_scalar(out, a, s1, s2, op0, op1))

    def stt(self, out, a, s, b, op0, op1, *w):
        self.wait(*w)
        return self.inc(self.e.scalar_tensor_tensor(out=out, in0=a, scalar=s, in1=b, op0=op0, op1=op1))

    def copy(self, out, a, *w):
        self.wait(*w)
        return self.inc(self.e.tensor_copy(out, a))

    def act(self, out, a, f, *w, bias=0.0, scale=1.0, accum=None):
        self.wait(*w)
        if accum is None:
            return self.inc(self.e.activation(out, a, f, bias=bias, scale=scale))
        return self.inc(self.e.activation(out, a, f, bias=bias, scale=scale, accum_out=accum))


class Slot:

    def __init__(self, ap):
        self.ap, self.free, self.was = ap, (), ()


class Ring:

    def __init__(self, aps):
        self.slots, self.i = [Slot(a) for a in aps], 0

    def take(self):
        s = self.slots[self.i % len(self.slots)]
        self.i += 1
        assert s.free is not None, "taken again before its readers are known"
        s.was, s.free = s.free, None
        return s


class Dma:

    def __init__(self, new_sem):
        self.new_sem, self.count, self.stores = new_sem, {}, []

    def start(self, eng, key, out, in_, *w, store=False):
        eng.wait(*w)
        if key not in self.count:
            self.count[key] = [self.new_sem(f"dma_{key}"), 0]
        c = self.count[key]
        c[1] += 16
        eng.e.dma_start(out, in_).then_inc(c[0], 16)
        if store:
            self.stores.append((c[0], c[1]))
        return (c[0], c[1])


STEPS = {}


def interleave(*streams):
    live = [[name, gen, 0, STEPS.get(name, 20)] for name, gen in streams if gen is not None]
    while live:
        s = min(live, key=lambda s: s[2] / s[3])
        if next(s[1], "end") == "end":
            STEPS[s[0]] = max(s[2], 1)
            live.remove(s)
        s[2] += 1


class Core:

    def __init__(self, nc, ctx, ins, spans, at):
        self.nc, self.ctx, self.ins, self.table = nc, ctx, ins, None
        sem = lambda n: ctx.enter_context(nc.semaphore(n))
        self.pe = Engine(nc.tensor, sem("pe_done"))
        self.act = Engine(nc.scalar, sem("act_done"))
        self.dve = Engine(nc.vector, sem("dve_done"))
        self.pool = Engine(nc.gpsimd, sem("pool_done"))
        self.sp = Engine(nc.sync, sem("sp_done"))
        self.dma = Dma(sem)
        self.bank = [ctx.enter_context(nc.psum_tensor(f"bank{i}", [P, 512], F32)) for i in range(8)]
        sb = lambda n, w, dt=F32: ctx.enter_context(nc.sbuf_tensor(n, [P, w], dt))
        whole = lambda n: sb(n, KC * T)[:, :].rearrange("p (c t) -> p c t", c=KC)
        at_byte = nc.sbuf_base
        self.hT, self.hT_cut = whole("hT"), self.second_name("hT_cut", KC * T, at_byte, KC)
        at_byte = nc.sbuf_base
        self.oT, self.oT_cut = whole("oT"), self.second_name("oT_cut", KC * T, at_byte, KC)
        self.spans, self.at = spans, at
        self.tables = {"common": sb("common_table", spans["common"][1])[:, :]}
        self.columns = sb("feature_cols", COLUMNS["lb"][0] + COLUMNS["lb"][1])
        self.eps_at = {e: i for i, e in enumerate((EPS, 4 * EPS, GN_EPS, NINE_LN2, 1.0, -0.5))}
        self.eps = sb("eps", 8)
        for e, i in self.eps_at.items():
            self.pool.inc(nc.gpsimd.memset(self.eps[:, i:i + 1], e))
        self.arena_words = 23784
        at_byte = nc.sbuf_base
        self.arena = sb("arena", self.arena_words)
        self.arena_cut = self.second_name("arena_cut", self.arena_words, at_byte, 1)[:, 0, :]
        self.used = 0

    def second_name(self, name, words, at_byte, blocks):
        t = self.nc.alloc_sbuf_tensor_at(name, [P, words], F32R, offset=-(-at_byte // 32) * 32)
        return t[:, :].rearrange("p (c t) -> p c t", c=blocks)

    def c(self, name, phase="common"):
        o, w = self.at[phase][name]
        return self.tables[phase][:, o:o + w]

    def load_table(self, phase):
        o, w = self.spans[phase]
        self.tables[phase] = self.room(w)
        self.dve.wait(self.load(f"table_{phase}", self.tables[phase], self.ins["table"][:, o:o + w]))

    def eps_col(self, e):
        i = self.eps_at[e]
        return self.eps[:, i:i + 1]

    def room(self, words):
        a = self.arena[:, self.used:self.used + words]
        self.used += words
        assert self.used <= self.arena_words, self.used
        return a

    def room_cut(self, words):
        at = self.used
        return self.room(words), self.arena_cut[:, at:at + words]

    def new_phase(self):
        every = [(e.sem, e.n) for e in (self.pe, self.act, self.dve, self.pool) if e.n]
        every += [(c[0], c[1]) for c in self.dma.count.values()]
        for e in (self.pe, self.act, self.dve, self.pool, self.sp):
            e.wait(*every)
        self.used, self.table = 0, None
        return Ring([b[:, :] for b in self.bank])

    def load(self, key, out, in_, *w):
        return self.dma.start(self.sp, key, out, in_, *w)

    def load_constants(self):
        o, w = self.spans["common"]
        self.load("common_table", self.tables["common"], self.ins["table"][:, o:o + w])
        self.columns_ready = self.load("columns", self.columns[:, :], self.ins["columns"])

    def weights(self, name, w, c0, n):
        return w[:, c0:c0 + n].rearrange("(c p) n -> p c n", p=P)

    def vec(self, key, out, name):
        o, w = COLUMNS[name]
        return self.dve.copy(out, self.columns[:, o:o + w], self.columns_ready)

    def row(self, key, out, src):
        n = src.shape[0]
        return self.load(key, out, src.unsqueeze(0).broadcast_to([P, n]))

    def project(self, bank, w, col, g, *waits, m=P, width=G):
        pe = self.pe
        pe.wait(*waits, *bank.was)
        for c in range(KC):
            ins = self.nc.tensor.matmul(bank.ap[0:m, 0:width], w[:, c, col:col + m],
                                        self.hT[:, c, g * width:(g + 1) * width], start=(c == 0), stop=(c == KC - 1))
            if c % 2 and c < KC - 1:
                yield
        return pe.inc(ins)

    def split(self, x, x_cut, hi, engine, *w, more=()):
        t = self.act.act(hi, x, ACT.Copy, *w, *more)
        return engine.tt(x_cut, x, hi, ALU.subtract, t)

    def product(self, out, a, b, start, stop):
        mm = self.nc.tensor.matmul
        mm(out, a[0], b[0], start=start, stop=False)
        mm(out, a[0], b[1], start=False, stop=False)
        return mm(out, a[1], b[0], start=False, stop=stop)

    def project_now(self, *args, **kw):
        gen = self.project(*args, **kw)
        while True:
            try:
                next(gen)
            except StopIteration as end:
                return end.value

    def ln(self, out, a, *w, **kw):
        if self.table != "ln":
            self.nc.scalar.preload_act_table_set("natural_log_exp_and_others")
            self.table = "ln"
        return self.act.act(out, a, ACT.Ln, *w, **kw)

    def tanh(self, out, a, *w, **kw):
        self.table = "tanh"
        return self.act.act(out, a, ACT.Tanh, *w, **kw)

    def norm_rows(self, x, junk, st, n, *w):
        a, v = self.act, self.dve
        t = a.act(junk, x, ACT.Square, *w, accum=st[:, n:n + 1])
        t = v.ts(st[:, n + 1:n + 2], st[:, n:n + 1], 1.0 / D, EPS, ALU.mult, ALU.add, t)
        return self.pool.tt(st[:, n + 2:n + 3], st[:, n + 1:n + 2], self.eps_col(-0.5), ALU.pow, t)

    def to_hT(self, psum, h, tile, nw, *w):
        pe, v = self.pe, self.dve
        wrote = []
        for half in range(2):
            b = psum.take()
            pe.wait(*w, *b.was)
            for j in range(4):
                c = 4 * half + j
                ins = self.nc.tensor.transpose(b.ap[:, j * P:(j + 1) * P], h[:, c * P:(c + 1) * P], self.c("ident"))
            t = pe.inc(ins)
            t2 = v.tt(self.hT[:, 4 * half:4 * half + 4, tile * P:(tile + 1) * P],
                      b.ap.rearrange("p (c t) -> p c t", c=4),
                      bc(nw[:, 4 * half:4 * half + 4], 2, P), ALU.mult, t)
            b.free = (t2,)
            wrote.append(t2)
        return t, wrote[-1]


def first_norm(k, psum):
    space = lambda i: k.oT[:, i, T // 2:]
    nw, st = k.room(KC), k.room(8)
    nw_ready = k.vec("nw", nw, "pre0")
    xr, hr = Ring([space(0), space(1)]), Ring([space(2), space(3)])
    scaled, pending = [], None
    load = lambda t, slot: k.load(f"x{t % 2}", slot.ap, k.ins["x"][0, t * P:(t + 1) * P, :], *slot.was)
    ahead = []
    for t in range(2):
        x = xr.take()
        ahead.append((x, load(t, x)))
    yield None
    k.dve.wait(nw_ready)
    for t in range(NT):
        (x, got), h = ahead.pop(0), hr.take()
        r = k.norm_rows(x.ap, h.ap, st, 4 * (t % 2), got, *h.was, *(scaled[t - 2:t - 1] if t >= 2 else ()))
        scaled.append(k.dve.ts(h.ap, x.ap, st[:, 4 * (t % 2) + 2:4 * (t % 2) + 3], None, ALU.mult, None, r))
        x.free = (scaled[-1],)
        if t + 2 < NT:
            x = xr.take()
            ahead.append((x, load(t + 2, x)))
        wrote = None
        if pending is not None:
            read, wrote = k.to_hT(psum, pending[0].ap, t - 1, nw, pending[1])
            pending[0].free = (read,)
        pending = (h, scaled[-1])
        yield wrote
    read, wrote = k.to_hT(psum, pending[0].ap, NT - 1, nw, pending[1])
    pending[0].free = (read,)
    yield wrote


def finish_layer(k, layer, x_in, x_out, w_out, bias, post_w, next_w, last_w):
    psum = k.new_phase()
    v, a, pe = k.dve, k.act, k.pe
    (wo, wo_lo), (_, wo_hi) = ([x.rearrange("p (c n) -> p c n", c=KC) for x in k.room_cut(KC * D)] for _ in range(2))
    got_w = [k.load(f"wo{c}", wo[:, c, :], w_out[c * P:(c + 1) * P, :]) for c in range(KC)]
    got_w = [k.split(wo[:, c, :], wo_lo[:, c, :], wo_hi[:, c, :], v, got_w[c]) for c in range(KC)]
    ready = []
    if bias is not None:
        b_row = k.room(D)
        ready.append(k.row("b_row", b_row, bias))
    if post_w is not None:
        p_row = k.room(D)
        ready.append(k.row("p_row", p_row, post_w))
    if last_w is not None:
        l_row = k.room(D)
        ready.append(k.row("l_row", l_row, last_w))
    if next_w is not None:
        nw = k.room(KC)
        ready.append(k.vec("nw", nw, next_w))
    xr = Ring([k.room(D) for _ in range(2)])
    yr = Ring([k.room(D) for _ in range(2)])
    jr = Ring([k.room(D)])
    st = k.room(16)
    v.wait(*ready)

    def tile(t):
        x = xr.take()
        got = k.load(f"x{t % 2}", x.ap, x_in[t * P:(t + 1) * P, :], *x.was)
        s0 = 8 * (t % 2)
        banks = []
        for n in range(2):
            b = psum.take()
            pe.wait(*b.was)
            for c in range(KC):
                pe.wait(got_w[c], cut[t])
                ins = k.product(b.ap, (k.hT_cut[:, c, t * P:(t + 1) * P], k.oT_cut[:, c, t * P:(t + 1) * P]),
                                (wo_hi[:, c, n * 512:(n + 1) * 512], wo_lo[:, c, n * 512:(n + 1) * 512]),
                                start=(c == 0), stop=(c == KC - 1))
            banks.append((b, pe.inc(ins)))
        yield
        y, junk = yr.take(), jr.take()
        done = []
        for n, (b, mm) in enumerate(banks):
            ysl = y.ap[:, n * 512:(n + 1) * 512]
            if bias is not None:
                b.free = (v.tt(ysl, b.ap, b_row[:, n * 512:(n + 1) * 512], ALU.add, mm, *y.was),)
            else:
                b.free = (a.act(ysl, b.ap, ACT.Copy, mm, *y.was),)
            done += b.free
        if post_w is not None:
            r = k.norm_rows(y.ap, junk.ap, st, s0, *done, *junk.was)
            scaled = v.stt(y.ap, y.ap, st[:, s0 + 2:s0 + 3], p_row, ALU.mult, ALU.mult, r)
        else:
            scaled = done[-1]
            v.wait(*done, *junk.was)
        new = v.tt(x.ap, x.ap, y.ap, ALU.add, scaled, got)
        yield
        r = k.norm_rows(x.ap, y.ap, st, s0 + 4, new)
        if last_w is not None:
            o = v.stt(junk.ap, x.ap, st[:, s0 + 6:s0 + 7], l_row, ALU.mult, ALU.mult, r, *junk.was)
            stored = k.dma.start(k.sp, f"out{t % 2}", x_out[t * P:(t + 1) * P, :], junk.ap, o, store=True)
            x.free, y.free, junk.free = (o,), (r,), (stored,)
            yield
            return
        stored = k.dma.start(k.sp, f"out{t % 2}", x_out[t * P:(t + 1) * P, :], x.ap, new, store=True)
        o = v.ts(junk.ap, x.ap, st[:, s0 + 6:s0 + 7], None, ALU.mult, None, r)
        yield
        read, _ = k.to_hT(psum, junk.ap, t, nw, o)
        x.free, y.free, junk.free = (o, stored), (r,), (read,)

    part = lambda t: k.split(*(x[:, :, t * P:(t + 1) * P] for x in (k.oT, k.oT_cut, k.hT_cut)), k.pool)
    cut = [part(0), part(1)]
    pending = None
    for t in range(NT):
        if t + 2 < NT:
            cut.append(part(t + 2))
        g = tile(t)
        next(g)
        if pending is not None:
            for _ in pending:
                pass
        pending = g
    for _ in pending:
        pass


def rope_tables(k, cos, sin, tmp, pos_i, got):
    v, a = k.dve, k.act
    n = NT * RH
    pos, ang, turn, red = (tmp[:, i * n:(i + 1) * n] for i in range(4))
    t = v.copy(pos[:, 0:NT], pos_i, got)
    t = v.tt(ang.rearrange("p (n f) -> p n f", f=RH), k.c("freq", "attention").rearrange("p (n f) -> p n f", f=RH),
             bc(pos[:, 0:NT], 2, RH), ALU.mult, t)
    two_pi = 2.0 * np.pi
    hi = float(np.float32(6.28125))
    mid = float(np.round((two_pi - hi) * 2.0 ** 20) / 2.0 ** 20)
    low = float(two_pi - hi - mid)
    magic = float(1.5 * 2.0 ** 23)
    for out, quarter in ((sin, 0.0), (cos, 0.25)):
        t = v.ts(turn, ang, float(1.0 / two_pi), quarter, ALU.mult, ALU.add, t)
        t = v.ts(turn, turn, magic, -magic, ALU.add, ALU.add, t)
        t = v.stt(red, turn, -hi, ang, ALU.mult, ALU.add, t)
        t = v.stt(red, turn, -mid, red, ALU.mult, ALU.add, t)
        t = v.stt(red, turn, -low, red, ALU.mult, ALU.add, t)
        t = v.ts(red, red, float(quarter * two_pi), float(np.float32(np.pi) - np.float32(1e-6)), ALU.add, ALU.min, t)
        t = v.ts(red, red, -float(np.float32(np.pi) - np.float32(1e-6)), None, ALU.max, None, t)
        t = a.act(out, red, ACT.Sin, t)
    return t


def attention(k):
    psum = k.new_phase()
    v, a, pe, pool = k.dve, k.act, k.pe, k.pool
    nc = k.nc
    w_in = k.ins["attn_w_in"][0]
    norms = first_norm(k, psum)
    next(norms)
    b_row = k.room(QKV)
    got_b = k.row("b_row", b_row, k.ins["attn_b_in"][0, 0:QKV])
    sinks = k.room(NH)
    got_s = k.row("sinks", sinks, k.ins["attn_sinks"][0])
    cs, sn = k.room(NT * RH), k.room(NT * RH)
    pos_i = k.oT[:, 6, T // 2:T // 2 + NT].bitcast(I32)
    got_p = k.load("pos", pos_i, k.ins["positions"])
    k.load_table("attention")
    wq = k.room(KC * QKV).rearrange("p (c n) -> p c n", c=KC)
    got_w = [k.load(f"wq{c}", wq[:, c], w_in[c * P:(c + 1) * P, 0:QKV]) for c in range(KC)]
    tables = rope_tables(k, cs, sn, k.oT[:, 7, :], pos_i, got_p)
    csv, snv = (x.rearrange("p (n f) -> p n f", f=RH) for x in (cs, sn))
    k_pair = [k.room(NKV * 2 * P).rearrange("p (g s t) -> p g s t", g=NKV, s=2) for _ in range(2)]
    v_keep = k.room(3 * P).rearrange("p (n d) -> p n d", n=3)
    qkv = Ring([k.room(QKV)])
    kd = Ring([k.room(2 * P)])
    ab = k.room(2 * 18 * ROPE)
    qT = Ring([k.room(8 * P)])
    prob = Ring([k.room(QUAD * 2 * P) for _ in range(2)])
    probT = Ring([k.room(QUAD * 2 * P) for _ in range(2)])
    stat = Ring([k.room(6 * QUAD) for _ in range(3)])
    normed = []
    next(norms)
    normed += [next(norms), next(norms)]
    v.wait(got_b, got_s, tables)
    last = {"scores": (), "pv": ()}
    made = {}

    def qkv_tile(t):
        x = qkv.take()
        done = []
        for c0, n in ((0, 512), (512, 512), (1024, 256)):
            b = psum.take()
            pe.wait(normed[t], *b.was)
            for c in range(KC):
                pe.wait(got_w[c])
                ins = nc.tensor.matmul(b.ap[:, 0:n], k.hT[:, c, t * P:(t + 1) * P], wq[:, c, c0:c0 + n],
                                       start=(c == 0), stop=(c == KC - 1))
                if c % 2 and c < KC - 1:
                    yield
            mm = pe.inc(ins)
            d = v.tt(x.ap[:, c0:c0 + n], b.ap[:, 0:n], b_row[:, c0:c0 + n], ALU.add, mm, *x.was)
            b.free = (d,)
            done.append(d)
            yield
        vv = a.act(v_keep[:, t % 3, :], x.ap[:, V0:V0 + P], ACT.Copy, *done, *last["pv"])
        heads = x.ap[:, 0:V0].rearrange("p (h d) -> p h d", d=HD)
        x12 = heads[:, :, 0:ROPE].rearrange("p h (a f) -> p h a f", a=2)
        pa = ab[:, 0:18 * ROPE].rearrange("p (h a f) -> p h a f", a=2, f=RH)
        pb = ab[:, 18 * ROPE:].rearrange("p (h a f) -> p h a f", a=2, f=RH)
        cb = bc(csv[:, t, :], 1, 18)
        sb = bc(snv[:, t, :], 1, 18)
        for i in range(2):
            ta = v.tt(pa[:, :, i, :], x12[:, :, i, :], cb, ALU.mult, *done)
            tb = v.tt(pb[:, :, i, :], x12[:, :, i, :], sb, ALU.mult)
        r1 = v.tt(x12[:, :, 0, :], pa[:, :, 0, :], pb[:, :, 1, :], ALU.subtract, tb)
        r2 = v.tt(x12[:, :, 1, :], pa[:, :, 1, :], pb[:, :, 0, :], ALU.add, tb)
        kk = kd.take()
        dup = v.copy(kk.ap.rearrange("p (g r d) -> p g r d", g=2, r=2),
                     bc(x.ap[:, KV0:KV0 + P].rearrange("p (g d) -> p g d", g=2), 2, 2),
                     r2, *kk.was)
        yield
        q = qT.take()
        outs = []
        for half in range(2):
            b = psum.take()
            pe.wait(r2, *b.was)
            for j in range(4):
                blk = 4 * half + j
                ins = nc.tensor.transpose(b.ap[:, j * P:(j + 1) * P], x.ap[:, blk * P:(blk + 1) * P], k.c("ident"))
            tr = pe.inc(ins)
            o = a.act(q.ap[:, half * 512:(half + 1) * 512], b.ap, ACT.Copy, tr, *q.was)
            b.free = (o,)
            outs.append(o)
        b = psum.take()
        pe.wait(dup, *b.was)
        for g in range(2):
            ins = nc.tensor.transpose(b.ap[:, g * P:(g + 1) * P], kk.ap[:, g * P:(g + 1) * P], k.c("ident"))
        tr = pe.inc(ins)
        kv = b.ap[:, 0:2 * P].rearrange("p (g t) -> p g t", g=2)
        o = a.act(k_pair[t % 2][:, :, 1, :], kv, ACT.Copy, tr, *last["scores"])
        o = a.act(k_pair[(t + 1) % 2][:, :, 0, :], kv, ACT.Copy)
        b.free = (o,)
        kk.free = (tr,)
        x.free = (vv, tr)
        made[t] = (q, outs[-1], o, vv)
        yield

    def views(u):
        t, g, quad = u // 4, u // 2 % 2, u % 2
        return t, g, quad, P if t == 0 else 0

    run = {}

    def scores(u):
        t, g, quad, lo = views(u)
        q, q_ready, k_ready, _ = made[t]
        p, st = prob.take(), stat.take()
        mx, ng, rs, se, dn, rc = (st.ap[:, i * QUAD:(i + 1) * QUAD] for i in range(6))
        pv4 = p.ap.rearrange("p (h w) -> p h w", h=QUAD)
        banks = [psum.take(), psum.take()]
        pe.wait(q_ready, k_ready, *banks[0].was, *banks[1].was)
        for j in range(2):
            for par in range(2):
                blk = 4 * g + 2 * quad + j
                rows = slice(64 * par, 64 * par + 64)
                ins = nc.tensor.matmul(banks[par].ap[:, j * 256 + lo:(j + 1) * 256],
                                       q.ap[rows, blk * P:(blk + 1) * P],
                                       k_pair[t % 2][rows, g, lo // P:2, :], start=True, stop=True)
        mm = pe.inc(ins)
        last["scores"] = (mm,)
        if u % 4 == 3:
            q.free = (mm,)
        h0 = GRP * g + QUAD * quad
        v.wait(mm, *p.was, *st.was)
        for par in range(2):
            for j in range(2):
                h = 2 * j + par
                m = v.inc(nc.vector.tensor_tensor_reduce(
                    out=pv4[:, h, lo:], in0=banks[par].ap[:, j * 256 + lo:(j + 1) * 256],
                    in1=k.c("band", "attention")[:, lo:], scale=HD ** -0.5, scalar=sinks[:, h0 + h:h0 + h + 1],
                    op0=ALU.add, op1=ALU.max, accum_out=mx[:, h:h + 1]))
            banks[par].free = (m,)
        n1 = v.ts(ng, mx, -1.0, None, ALU.mult, None, m)
        n2 = v.tt(se, sinks[:, h0:h0 + QUAD], mx, ALU.subtract, m)
        for h in range(QUAD):
            e = a.act(pv4[:, h, lo:], pv4[:, h, lo:], ACT.Exp, n1, bias=ng[:, h:h + 1], accum=rs[:, h:h + 1])
        e2 = a.act(se, se, ACT.Exp, n2)
        run[u] = (p, pv4, st, rs, se, dn, rc, e, e2)

    def divide(u):
        _, _, _, lo = views(u)
        p, pv4, st, rs, se, dn, rc, e, e2 = run[u]
        d = v.tt(dn, rs, se, ALU.add, e, e2)
        v.wait(d)
        d = v.inc(nc.vector.reciprocal(rc, dn))
        for h in range(QUAD):
            d = v.ts(pv4[:, h, lo:], pv4[:, h, lo:], rc[:, h:h + 1], 0.5, ALU.mult, ALU.mult, d if h == 0 else e)
        st.free = (d, e, e2)
        run[u] = (p, pv4, d)

    def turn(u):
        t, g, quad, _ = views(u)
        p, pv4, d = run[u]
        pt = probT.take()
        ptv = pt.ap.rearrange("p (s h q) -> p s h q", s=2, h=QUAD)
        evs = []
        for s in range(0 if t else 1, 2):
            b = psum.take()
            pe.wait(d, *b.was)
            for j in range(QUAD):
                ins = nc.tensor.transpose(b.ap[:, j * P:(j + 1) * P], pv4[:, j, s * P:(s + 1) * P], k.c("ident"))
            tr = pe.inc(ins)
            evs.append(a.act(ptv[:, s], b.ap.rearrange("p (h q) -> p h q", h=QUAD), ACT.Copy, tr, *pt.was))
            b.free = (evs[-1],)
        p.free = (tr,)
        run[u] = (pt, ptv, evs)

    def values(u):
        t, g, quad, _ = views(u)
        pt, ptv, evs = run.pop(u)
        v_ready = made[t][3]
        first = 0 if t else 1
        b = psum.take()
        pe.wait(*evs, v_ready, *b.was)
        pair = ptv.rearrange("p s (j r) q -> p s r j q", r=2)
        for par in range(2):
            for s in range(first, 2):
                ins = nc.tensor.matmul(b.ap[64 * par:64 * par + 64, 0:2 * P], v_keep[:, (t - 1 + s) % 3, g * HD:(g + 1) * HD],
                                       pair[:, s, par, :, :], start=(s == first), stop=(s == 1))
        mm = pe.inc(ins)
        last["pv"] = (mm,)
        blk = 4 * g + 2 * quad
        if t == NT // 2:
            v.wait(normed[-1])
        o = v.copy(k.oT[:, blk:blk + 2, t * P:(t + 1) * P], b.ap[:, 0:2 * P].rearrange("p (j q) -> p j q", j=2), mm)
        b.free = (o,)
        pt.free = (mm,)

    for _ in qkv_tile(0):
        pass
    ahead = None
    for u in range(-2, 4 * NT + 1):
        step = (u + 2) % 4
        if step == 0:
            ahead = qkv_tile((u + 2) // 4 + 1) if (u + 2) // 4 + 1 < NT else None
        if len(normed) < NT:
            normed.append(next(norms))
        if 0 <= u < 4 * NT:
            turn(u)
        if ahead is not None and step < 3:
            next(ahead)
            next(ahead)
        if -1 <= u < 4 * NT - 1:
            divide(u + 1)
        if u >= 1:
            values(u - 1)
        if u + 2 < 4 * NT:
            scores(u + 2)
        if ahead is not None:
            for _ in range((2, 2, 3)[step] if step < 3 else 9):
                next(ahead, None)


def attention_gate(k):
    psum = k.new_phase()
    v, pe = k.dve, k.pe
    w_in = k.ins["attn_w_in"][0]
    wz = Ring([k.room_cut(2 * KC * P) for _ in range(2)])
    th = Ring([k.room(G) for _ in range(2)])
    u = Ring([k.room(G) for _ in range(2)])
    h_hi = k.room_cut(KC * T)[1].rearrange("p (c t) -> p c t", c=KC)
    zb, hb = k.room(KC), k.room(KC)
    b = k.vec("zb", zb, "att_zb")
    half = v.ts(hb, zb, 0.5, None, ALU.mult, None, b)
    cut = {}

    def load_columns(f):
        w = wz.take()
        raw, w3 = (x.rearrange("p (i c n) -> p i c n", i=2, c=KC) for x in w.ap)
        got = k.load(f"wz{f % 2}", raw[:, 0], k.weights("z", w_in, Z0 + f * P, P), *w.was)
        return w, w3, k.split(raw[:, 0], w3[:, 0], w3[:, 1], k.pool, got, more=w.was)

    ahead = load_columns(0)
    for f in range(KC):
        w, w3, got = ahead
        for g in range(NG):
            if f == 0:
                cols = slice(g * G, (g + 1) * G)
                for c in range(KC):
                    cut[c, g] = k.split(k.hT[:, c, cols], k.hT_cut[:, c, cols], h_hi[:, c, cols], v)
            if g == 1 and f + 1 < KC:
                ahead = load_columns(f + 1)
            bk, tb, ub = psum.take(), th.take(), u.take()
            pe.wait(got, *bk.was)
            for c in range(KC):
                pe.wait(cut[c, g])
                ins = k.product(bk.ap, (w3[:, 1, c, :], w3[:, 0, c, :]),
                                (h_hi[:, c, g * G:(g + 1) * G], k.hT_cut[:, c, g * G:(g + 1) * G]),
                                start=(c == 0), stop=(c == KC - 1))
            mm = pe.inc(ins)
            t1 = k.tanh(tb.ap, bk.ap, mm, half, *tb.was, bias=hb[:, f:f + 1], scale=0.5)
            o = k.oT[:, f, g * G:(g + 1) * G]
            t2 = v.stt(ub.ap, bk.ap, zb[:, f:f + 1], o, ALU.add, ALU.mult, t1, *ub.was)
            t3 = v.stt(o, tb.ap, 1.0, ub.ap, ALU.add, ALU.mult, t1, t2)
            bk.free, tb.free, ub.free = (t2,), (t3,), (t3,)
        w.free = (mm,)


def recurrence(k):
    psum = k.new_phase()
    front_banks, back_banks = Ring([s.ap for s in psum.slots[0:4]]), Ring([s.ap for s in psum.slots[4:8]])
    v, a, pe, pool, nc = k.dve, k.act, k.pe, k.pool, k.nc
    w_in = k.ins["rec_w_in"][0]
    heads = D // RK
    w_r = [Ring([k.room_cut(2 * KC * RK)]) for _ in range(4)]
    two = lambda: Ring([k.room(G) for _ in range(2)])
    one = lambda: Ring([k.room(G)])
    q_r, k_r, b_r, z_r, v_r = two(), two(), two(), two(), two()
    th_r, tf_r = two(), one()
    lg_r = one()
    d_r, e_r = (Ring([k.room(G) for _ in range(3)]) for _ in range(2))
    st_r = one()
    eb_r, qt_r, kt_r = one(), one(), one()
    first_e = one()
    sq_r, rs_r = e_r, d_r
    state = Ring([k.room(RK) for _ in range(5)])
    k.load_table("recurrence")
    width = LEVELS * G // 2
    sel = k.room(width // 4).bitcast(I8)
    sel_ok = v.copy(sel, k.oT[:, 0, 0:width], k.load("select", k.oT[:, 0, 0:width], k.ins["select"]))
    kept = k.room(heads * RK)
    lb = k.room(8 * KC)
    l0, l1, lm, bb, ab, nb = (lb[:, i * KC:(i + 1) * KC] for i in range(6))
    gn = k.room(1)
    t0 = k.vec("lb0", l0, "lb0")
    t1 = k.vec("lb1", l1, "lb1")
    t2 = k.vec("gn", gn, "rec_gn")
    g_half = v.ts(gn, gn, 0.5, None, ALU.mult, None, t2)
    m = v.tt(lm, l0, l1, ALU.max, t0, t1)
    x0 = v.tt(l0, l0, lm, ALU.subtract, m)
    x1 = v.tt(l1, l1, lm, ALU.subtract, m)
    x0 = a.act(l0, l0, ACT.Exp, x0)
    x1 = a.act(l1, l1, ACT.Exp, x1)
    m = v.tt(lm, l0, l1, ALU.add, x0, x1)
    v.wait(m)
    m = v.inc(nc.vector.reciprocal(lm, lm))
    x1 = v.tt(l1, l1, lm, ALU.mult, m)
    x2 = v.ts(bb, l1, -0.5, 0.5, ALU.mult, ALU.add, x1)
    x3 = v.ts(nb, bb, -1.0, None, ALU.mult, None, x2)
    x4 = v.ts(ab, l1, 1e-7, None, ALU.max, None, x1)
    bounds = v.tt(ab, ab, bb, ALU.add, x4, x2)
    v.wait(x3)
    made = {}

    hi_of = lambda g: (k.oT_cut if g < NG // 2 else k.hT_cut)[:, :, ((g + NG // 2) % NG) * G:((g + NG // 2) % NG + 1) * G]
    cols = lambda g: slice(g * G, (g + 1) * G)
    cut, piece, coming, last_read = {}, {}, {}, []
    visits = [(half, h) for half in range(2) for h in range(heads)]

    def start_load(i, visit, *w):
        slot = w_r[i].take()
        raw, w3 = (x.rearrange("p (s c n) -> p s c n", s=2, c=KC) for x in slot.ap)
        h = visits[visit][1]
        coming[i] = (slot, raw, w3, k.load(f"wr{i}", raw[:, 0], k.weights("", w_in, i * D + h * RK, RK), *slot.was))

    def end_load(i):
        if i in coming:
            slot, raw, w3, got = coming.pop(i)
            piece[i] = (slot, (w3[:, 1], w3[:, 0]), k.split(raw[:, 0], w3[:, 0], w3[:, 1], pool, got, more=slot.was))

    def project(i, bank, g):
        _, (w_hi, w_lo), w_ok = piece[i]
        h_hi = hi_of(g)
        pe.wait(w_ok, *bank.was)
        for c in range(KC):
            pe.wait(cut[c, g])
            ins = k.product(bank.ap, (w_hi[:, c, :], w_lo[:, c, :]), (h_hi[:, c, :], k.hT_cut[:, c, cols(g)]),
                            start=(c == 0), stop=(c == KC - 1))
            if c < KC - 1:
                yield
        return pe.inc(ins)

    def used(i, visit, g, mm):
        if g % 2:
            piece[i][0].free = (mm,)
            if visit + 1 < len(visits):
                start_load(i, visit + 1)

    view = lambda ap, H: ap.rearrange("p (n a i) -> p n a i", a=2, i=H)

    def factors(l, q, kk, b, q_ok, k_ok, b_ok, e_r):
        H = 1 << l
        d, e = d_r.take(), e_r.take()
        bv4, d4, e4 = view(b.ap, H), view(d.ap, H), view(e.ap, H)
        ref = bc(bv4[:, :, 0, H - 1], 2, H)
        d1 = pool.tt(d4[:, :, 0, :], ref, bv4[:, :, 0, :], ALU.subtract, b_ok, *d.was)
        d2 = pool.tt(d4[:, :, 1, :], bv4[:, :, 1, :], ref, ALU.subtract)
        x = a.act(d.ap, d.ap, ACT.Exp, d1, d2)
        e1 = v.tt(e4[:, :, 0, :], d4[:, :, 0, :], view(kk.ap, H)[:, :, 0, :], ALU.mult, x, k_ok, *e.was)
        e2 = v.tt(e4[:, :, 1, :], d4[:, :, 1, :], view(q.ap, H)[:, :, 1, :], ALU.mult, q_ok)
        d.free = (e2,)
        return e, e1, e2

    def front(visit, g):
        h = visits[visit][1]
        if h == 0:
            for c in range(KC):
                cut[c, g] = k.split(k.hT[:, c, cols(g)], k.hT_cut[:, c, cols(g)], hi_of(g)[:, c, :], v, sel_ok, *last_read)
        q, z = q_r.take(), z_r.take()
        pairs = []
        for i, dst in ((0, q), (3, z)):
            bank, th = front_banks.take(), th_r.take()
            mm = yield from project(i, bank, g)
            end_load(2 if i == 0 else 0)
            used(i, visit, g, mm)
            yield
            pairs.append((bank, th, dst, mm))
        bf, tf = front_banks.take(), tf_r.take()
        mf = yield from project(1, bf, g)
        end_load(3)
        used(1, visit, g, mf)
        ts = [k.tanh(th.ap, bank.ap, mm, *th.was, scale=0.5) for bank, th, _, mm in pairs]
        t = k.tanh(tf.ap, bf.ap, mf, *tf.was, scale=0.5)
        bf.free = (t,)
        kk, lg, b = k_r.take(), lg_r.take(), b_r.take()
        t2 = k.ln(lg.ap, tf.ap, t, bounds, *lg.was, bias=ab[:, h:h + 1], scale=bb[:, h:h + 1])
        for _ in range(3):
            yield
        oks = []
        for (bank, th, dst, mm), x in zip(pairs, ts):
            ok = v.stt(dst.ap, th.ap, 1.0, bank.ap, ALU.add, ALU.mult, x, *dst.was)
            bank.free, th.free = (ok,), (ok,)
            oks.append(ok)
        q_ok, z_ok = oks
        k_ok = v.ts(kk.ap, tf.ap, nb[:, h:h + 1], bb[:, h:h + 1], ALU.mult, ALU.add, t, bounds, *kk.was)
        t = t2
        tf.free = (t, k_ok)
        v.wait(t, *b.was)
        b_ok = v.inc(nc.vector.tensor_tensor_scan(out=b.ap, data0=k.c("run128", "recurrence"), data1=lg.ap, initial=0.0,
                                                  op0=ALU.mult, op1=ALU.add))
        lg.free = (b_ok,)
        yield
        bv = front_banks.take()
        mv = yield from project(2, bv, g)
        end_load(1)
        used(2, visit, g, mv)
        last_read[:] = [mv]
        th = th_r.take()
        x = a.act(th.ap, bv.ap, ACT.Copy, mv, *th.was)
        bv.free = (x,)
        first = factors(0, q, kk, b, q_ok, k_ok, b_ok, first_e)
        yield
        bv = front_banks.take()
        pe.wait(x, *bv.was)
        for u in range(4):
            sl = slice(u * P, (u + 1) * P)
            ins = nc.tensor.transpose(bv.ap[:, sl], th.ap[:, sl], k.c("ident"))
        tr = pe.inc(ins)
        th.free = (tr,)
        vv = v_r.take()
        v_ok = a.act(vv.ap, bv.ap, ACT.Copy, tr, *vv.was)
        bv.free = (v_ok,)
        made[h, g] = (q, kk, b, z, vv, q_ok, k_ok, b_ok, z_ok, v_ok, first)
        yield

    carried = {}
    v4 = lambda ap: ap.rearrange("p (u t) -> p u t", u=4)

    def back(h, g):
        q, kk, b, z, vv, q_ok, k_ok, b_ok, z_ok, v_ok, first = made.pop((h, g))
        levels = lambda l: factors(l, q, kk, b, q_ok, k_ok, b_ok, e_r)
        ahead = [first, levels(1)]
        yield
        bk, sc = back_banks.take(), st_r.take()
        pe.wait(q_ok, k_ok, *bk.was)
        for u in range(4):
            sl = slice(u * P, (u + 1) * P)
            ins = nc.tensor.matmul(bk.ap[:, sl], kk.ap[:, sl], q.ap[:, sl], start=True, stop=True)
        mm = pe.inc(ins)
        s_ok = v.tt(v4(sc.ap), v4(bk.ap), bc(k.c("ident"), 1, 4), ALU.mult, mm, *sc.was)
        bk.free = (s_ok,)
        yield
        eb, qt, kt = eb_r.take(), qt_r.take(), kt_r.take()
        for l in range(LEVELS):
            H = 1 << l
            e, e1, e2 = ahead.pop(0)
            if l + 2 < LEVELS:
                ahead.append(levels(l + 2))
                yield
            elif l + 2 == LEVELS:
                d = d_r.take()
                x1 = a.act(eb.ap, b.ap, ACT.Exp, b_ok, *eb.was)
                qt_ok = v.tt(qt.ap, q.ap, eb.ap, ALU.mult, x1, *qt.was)
                q.free = (qt_ok, mm)
                d1 = pool.tt(v4(d.ap), bc(v4(b.ap)[:, :, P - 1], 2, P), v4(b.ap), ALU.subtract, *d.was)
                b.free = (d1, x1)
                x2 = a.act(d.ap, d.ap, ACT.Exp, d1)
                d2 = v.tt(d.ap, d.ap, kk.ap, ALU.mult, x2)
                kk.free = (d2, mm)
                yield
            bk = back_banks.take()
            pe.wait(e1, e2, *bk.was)
            for u in range(4):
                sl = slice(u * P, (u + 1) * P)
                ins = nc.tensor.matmul(bk.ap[:, u * CH:(u + 1) * CH], e.ap[:, sl], view(e.ap[:, sl], H)[:, :, 1, :],
                                       start=True, stop=True)
            mm2 = pe.inc(ins)
            e.free = (mm2,)
            v.wait(mm2, s_ok)
            s_ok = v.inc(nc.vector.copy_predicated(
                out=view(sc.ap, H)[:, :, 1, :],
                mask=sel[:, l * G // 2:(l + 1) * G // 2].rearrange("p (n i) -> p n i", i=H),
                data=bk.ap[:, 0:G // 2].rearrange("p (n i) -> p n i", i=H)))
            bk.free = (s_ok,)
            yield
        bk = back_banks.take()
        pe.wait(d2, *bk.was)
        for u in range(4):
            sl = slice(u * P, (u + 1) * P)
            ins = nc.tensor.transpose(bk.ap[:, sl], d.ap[:, sl], k.c("ident"))
        tr = pe.inc(ins)
        d.free = (tr,)
        kt_ok = v.copy(kt.ap, bk.ap, tr, *kt.was)
        bk.free = (kt_ok,)
        yield
        yield
        bs = back_banks.take()
        pe.wait(kt_ok, v_ok, *bs.was)
        for u in range(4):
            sl = slice(u * P, (u + 1) * P)
            ins = nc.tensor.matmul(bs.ap[:, sl], kt.ap[:, sl], vv.ap[:, sl], start=True, stop=True)
        ds = pe.inc(ins)
        kt.free = (ds,)
        olds = [carried.get(h)]
        for u in range(4):
            sl, old = slice(u * P, (u + 1) * P), olds[-1]
            if u == 3 and g == NG // 2 - 1:
                new = Slot(kept[:, h * RK:(h + 1) * RK])
            else:
                new = state.take()
            if old is None:
                s_new = v.copy(new.ap, bs.ap[:, sl], ds, *new.was)
            else:
                s_new = v.stt(new.ap, old[0].ap, eb.ap[:, u * P + P - 1:u * P + P], bs.ap[:, sl], ALU.mult, ALU.add,
                              ds, x1, old[1], *new.was)
            olds.append((new, s_new))
        bs.free, eb.free = (s_new,), (s_new, qt_ok)
        yield
        bo = back_banks.take()
        pe.wait(s_ok, qt_ok, *bo.was)
        for u in range(4):
            sl, old = slice(u * P, (u + 1) * P), olds[u]
            ins = nc.tensor.matmul(bo.ap[:, sl], vv.ap[:, sl], sc.ap[:, sl], start=True, stop=old is None)
            if old is not None:
                pe.wait(old[1])
                ins = nc.tensor.matmul(bo.ap[:, sl], old[0].ap, qt.ap[:, sl], start=False, stop=True)
            mo = pe.inc(ins)
            if old is not None:
                old[0].free = (mo, olds[u + 1][1])
            if u == 1:
                yield
        carried[h] = olds[4]
        if g == NG - 1:
            carried[h][0].free = (s_new,)
        sc.free, vv.free, qt.free = (mo,), (mo,), (mo,)
        yield
        yield from norm_over_features(k, bo, mo, back_banks, sq_r, rs_r, z, z_ok, gn, g_half, h, g, 4 * EPS)

    for i in (0, 3, 1, 2):
        start_load(i, 0)
    for i in (0, 3, 1, 2):
        end_load(i)
    units = [(visit, 2 * half + g) for visit, (half, h) in enumerate(visits) for g in range(2)]
    for _ in front(*units[0]):
        pass
    for i, (visit, g) in enumerate(units):
        ahead = front(*units[i + 1]) if i + 1 < len(units) else None
        interleave(("rec front", ahead), ("rec back", back(visits[visit][1], g)))


def norm_over_features(k, bo, mo, banks, sq_r, rs_r, z, z_ok, gn, g_half, block, g, eps):
    a, v, pe, nc = k.act, k.dve, k.pe, k.nc
    sq, rs = sq_r.take(), rs_r.take()
    x = a.act(sq.ap, bo.ap, ACT.Square, mo, *sq.was)
    yield
    bk = banks.take()
    pe.wait(x, *bk.was)
    mm = pe.inc(nc.tensor.matmul(bk.ap, k.c("ones"), sq.ap, start=True, stop=True))
    yield
    x = k.ln(rs.ap, bk.ap, mm, *rs.was, scale=1.0 / P, bias=k.eps_col(eps))
    bk.free = (x,)
    x = a.act(rs.ap, rs.ap, ACT.Exp, x, scale=-0.5)
    o = v.tt(sq.ap, bo.ap, rs.ap, ALU.mult, x, mm)
    bo.free, rs.free = (o,), (o,)
    o = v.stt(k.oT[:, block, g * G:(g + 1) * G], sq.ap, gn, z.ap, ALU.mult, ALU.mult, o, g_half, z_ok)
    sq.free, z.free = (o,), (o,)
    yield


def gla(k):
    psum = k.new_phase()
    fb, bb = Ring([s.ap for s in psum.slots[0:3]]), Ring([s.ap for s in psum.slots[3:8]])
    v, a, pe, pool, nc = k.dve, k.act, k.pe, k.pool, k.nc
    w_in = k.ins["w_in_2"][0]
    room = k.room
    k.load_table("gla")
    w_r = {name: Ring([room(KC * n)]) for name, n in (("q", P), ("k", P), ("v", 2 * P), ("z", 2 * P))}
    weights = {}
    wg = room(KC * 16).rearrange("p (c n) -> p c n", c=KC)
    low = room(T)
    up = room(256)
    bias, gn = room(2), room(1)
    got = [k.load("wg", wg, k.weights("", w_in, GLA_R, 16)),
           k.load("up", up[0:16, :], k.ins["gla_gate_up_2"][0]),
           k.vec("gb", bias, "gla_b"), k.vec("gn", gn, "gla_gn")]
    g_half = v.ts(gn, gn, 0.5, None, ALU.mult, None, got[3])
    v.wait(*got)
    a.wait(*got)
    def load_piece(p, name):
        c0, n = {"q": (GLA_Q, P), "k": (GLA_K, P), "v": (GLA_V, 2 * P), "z": (GLA_Z, 2 * P)}[name]
        w = w_r[name].take()
        wv = w.ap.rearrange("p (c n) -> p c n", c=KC)
        weights[name] = (w, wv, k.load(f"wgla_{name}", wv, k.weights("", w_in, c0 + p * n, n), *w.was))

    def used(p, g, name, mm):
        if g == NG - 1:
            weights[name][0].free = (mm,)
            if p == 0:
                load_piece(1, name)

    for name in "zqkv":
        load_piece(0, name)
    lows = []
    for g in range(NG):
        b = fb.take()
        mm = k.project_now(b, wg, 0, g, *got, m=16)
        t = a.act(low[0:16, g * G:(g + 1) * G], b.ap[0:16, :], ACT.Copy, mm)
        b.free = (t,)
        lows.append(t)
    one = lambda n=G: Ring([room(n)])
    tmp = Ring([room(G) for _ in range(3)])
    two = lambda n=G: Ring([room(n) for _ in range(2)])
    q_r, ki_r, ks_r, eb_r, v_r = two(), two(), two(), two(), two(2 * G)
    z_r = Ring([room(G) for _ in range(4)])
    b_r, kt_r, sc_r = one(), one(), two()
    st = one(9 * P)
    sq_r, rs_r = one(), one()
    v4 = lambda ap: ap.rearrange("p (u t) -> p u t", u=4)
    made = {}

    def front(p, g):
        wz, wq, wk, wv = (weights[name][1] for name in "zqkv")
        gz, gq, gk, gv = (weights[name][2] for name in "zqkv")
        zs = []
        for h in range(2):
            bz, th, z = fb.take(), tmp.take(), z_r.take()
            mz = yield from k.project(bz, wz, h * P, g, gz)
            t = k.tanh(th.ap, bz.ap, mz, *th.was, scale=0.5)
            zo = v.stt(z.ap, th.ap, 1.0, bz.ap, ALU.add, ALU.mult, t, *z.was)
            bz.free, th.free = (zo,), (zo,)
            zs.append((z, zo))
            yield
        used(p, g, "z", mz)
        bg = fb.take()
        pe.wait(lows[g], *bg.was)
        mg = pe.inc(nc.tensor.matmul(bg.ap, up[0:16, p * P:(p + 1) * P], low[0:16, g * G:(g + 1) * G],
                                     start=True, stop=True))
        t1, t2 = tmp.take(), tmp.take()
        read = a.act(t1.ap, bg.ap, ACT.Abs, mg, *t1.was, bias=bias[:, p:p + 1])
        x = a.act(t1.ap, t1.ap, ACT.Exp, read, scale=-1.0)
        x = k.ln(t1.ap, t1.ap, x, bias=1.0)
        y = v.ts(t2.ap, bg.ap, bias[:, p:p + 1], 0.0, ALU.add, ALU.min, mg, read, *t2.was)
        bg.free = (y,)
        y = v.tt(t2.ap, t2.ap, t1.ap, ALU.subtract, x, y)
        t1.free = (y,)
        b = b_r.take()
        v.wait(y, *b.was)
        b_ok = v.inc(nc.vector.tensor_tensor_scan(out=b.ap, data0=k.c("run64", "gla"), data1=t2.ap, initial=0.0,
                                                  op0=ALU.mult, op1=ALU.add))
        t2.free = (b_ok,)
        eb, en, es = eb_r.take(), tmp.take(), tmp.take()
        x1 = a.act(eb.ap, b.ap, ACT.Exp, b_ok, *eb.was, scale=1.0 / 16)
        x2 = a.act(en.ap, b.ap, ACT.Exp, b_ok, *en.was, scale=-1.0 / 16)
        c8 = lambda ap: ap.rearrange("p (n t) -> p n t", t=CH)
        x3 = pool.tt(c8(es.ap), bc(c8(b.ap)[:, :, CH - 1], 2, CH), c8(b.ap), ALU.subtract, b_ok, *es.was)
        x3 = a.act(es.ap, es.ap, ACT.Exp, x3, scale=1.0 / 16)
        b.free = (x1, x2, x3)
        bq = fb.take()
        mq = yield from k.project(bq, wq, 0, g, gq)
        used(p, g, "q", mq)
        q = q_r.take()
        q_ok = v.stt(q.ap, bq.ap, HD ** -0.5, eb.ap, ALU.mult, ALU.mult, mq, x1, *q.was)
        bq.free = (q_ok,)
        bk = fb.take()
        mk = yield from k.project(bk, wk, 0, g, gk)
        used(p, g, "k", mk)
        ki, ks = ki_r.take(), ks_r.take()
        ki_ok = v.tt(ki.ap, bk.ap, en.ap, ALU.mult, mk, x2, *ki.was)
        ks_ok = v.tt(ks.ap, bk.ap, es.ap, ALU.mult, mk, x3, *ks.was)
        bk.free, en.free, es.free = (ks_ok,), (ki_ok,), (ks_ok,)
        vv = v_r.take()
        vvv = vv.ap.rearrange("p (u n) -> p u n", u=4)
        for half in range(2):
            b2 = fb.take()
            pe.wait(gv, *b2.was)
            for u in range(2):
                t0 = g * G + (2 * half + u) * P
                for c in range(KC):
                    ins = nc.tensor.matmul(b2.ap[:, u * 256:(u + 1) * 256], k.hT[:, c, t0:t0 + P],
                                           wv[:, c, :], start=(c == 0), stop=(c == KC - 1))
                    if c == 3:
                        yield
            mm = pe.inc(ins)
            v_ok = a.act(vvv[:, 2 * half:2 * half + 2, :], b2.ap.rearrange("p (u n) -> p u n", u=2), ACT.Copy,
                         mm, *vv.was)
            b2.free = (v_ok,)
        used(p, g, "v", mm)
        yield
        made[p, g] = (q, q_ok, ki, ki_ok, ks, ks_ok, eb, vv, vvv, v_ok, zs)

    def back(p, g):
        q, q_ok, ki, ki_ok, ks, ks_ok, eb, vv, vvv, v_ok, zs = made.pop((p, g))
        b2, kt = bb.take(), kt_r.take()
        pe.wait(ks_ok, *b2.was)
        for u in range(4):
            ins = nc.tensor.transpose(b2.ap[:, u * P:(u + 1) * P], ks.ap[:, u * P:(u + 1) * P], k.c("ident"))
        tr = pe.inc(ins)
        ks.free = (tr,)
        kt_ok = a.act(kt.ap, b2.ap, ACT.Copy, tr, *kt.was)
        b2.free = (kt_ok,)
        yield
        scs, b2 = [], [bb.take(), bb.take()]
        pe.wait(q_ok, ki_ok, *b2[0].was, *b2[1].was)
        for u in range(4):
            for h in range(2):
                rows, sl = slice(64 * h, 64 * h + 64), slice(u * P, (u + 1) * P)
                ins = nc.tensor.matmul(b2[h].ap[:, sl], ki.ap[rows, sl], q.ap[rows, sl], start=True, stop=True)
        mm = pe.inc(ins)
        ki.free = (mm,)
        for h in range(2):
            sc = sc_r.take()
            s_ok = v.tt(v4(sc.ap), v4(b2[h].ap), bc(k.c("mask", "gla"), 1, 4), ALU.mult, mm, *sc.was)
            b2[h].free = (s_ok,)
            scs.append((sc, s_ok))
        yield
        b2 = [bb.take(), bb.take()]
        pe.wait(kt_ok, v_ok, *b2[0].was, *b2[1].was)
        kt3 = v4(kt.ap)
        for u in range(4):
            for c in range(2):
                for h in range(2):
                    rows = slice(64 * c, 64 * c + 64)
                    ins = nc.tensor.matmul(b2[c].ap[64 * h:64 * h + 64, u * P:(u + 1) * P],
                                           kt3[rows, u, 64 * h:64 * h + 64], vvv[rows, u, h * P:(h + 1) * P],
                                           start=True, stop=True)
        mm = pe.inc(ins)
        kt.free = (mm,)
        s = st.take()
        s3 = s.ap.rearrange("p (i n) -> p i n", n=P)
        if g == 0:
            v.wait(*s.was)
            last = v.inc(nc.vector.memset(s3[:, 0, :], 0.0))
        else:
            last = v.copy(s3[:, 0, :], s3[:, 8, :], *s.was)
        for i in range(8):
            last = v.stt(s3[:, i + 1, :], s3[:, i, :], eb.ap[:, i * CH + CH - 1:(i + 1) * CH],
                         b2[i % 2].ap[:, (i // 2) * P:(i // 2 + 1) * P], ALU.mult, ALU.add, last, mm)
        b2[0].free = b2[1].free = (last,)
        eb.free = (last, q_ok)
        yield
        yield
        outs = [bb.take(), bb.take()]
        pe.wait(last, *outs[0].was, *outs[1].was)
        for h in range(2):
            sc, s_ok = scs[h]
            pe.wait(s_ok)
            rows = slice(64 * h, 64 * h + 64)
            for u in range(4):
                sl = slice(u * P, (u + 1) * P)
                nc.tensor.matmul(outs[h].ap[:, sl], vvv[:, u, h * P:(h + 1) * P], sc.ap[:, sl],
                                 start=True, stop=False)
                for c in range(2):
                    t0 = u * P + c * CH
                    ins = nc.tensor.matmul(outs[h].ap[:, t0:t0 + CH], s3[rows, 2 * u + c, :],
                                           q.ap[rows, t0:t0 + CH], start=False, stop=(c == 1))
                if u == 1:
                    yield
            mo = pe.inc(ins)
            sc.free = (mo,)
            z, zo = zs[h]
            if h == 1:
                vv.free, s.free, q.free = (mo,), (mo,), (mo,)
            yield
            yield from norm_over_features(k, outs[h], mo, bb, sq_r, rs_r, z, zo, gn, g_half, 2 * p + h, g, EPS)

    units = [(p, g) for p in range(2) for g in range(NG)]
    for _ in front(0, 0):
        pass
    for i, unit in enumerate(units):
        ahead = front(*units[i + 1]) if i + 1 < len(units) else None
        interleave(("gla front", ahead), ("gla back", back(*unit)))


def delta_rule(k):
    psum = k.new_phase()
    fb, sb, vb, cb = (Ring([s.ap for s in psum.slots[2 * i:2 * i + 2]]) for i in range(4))
    v, a, pe, pool, nc = k.dve, k.act, k.pe, k.pool, k.nc
    w_in = k.ins["w_in_2"][0]
    room = k.room
    cst = lambda name: k.c(name, "delta")
    wr = Ring([room(4 * KC * P)])
    first_w = wr.take()
    first_wv = first_w.ap.rearrange("p (i c n) -> p i c n", i=4, c=KC)
    got_wa = k.load("wd", first_wv[:, 0], k.weights("", w_in, RW_WA, P))
    wa = room(T)
    up = room(512)
    cols = room(64)
    o0, off = COLUMNS["rwkv"]
    names = {n: COLUMNS[n][0] - o0 for n in ("mu", "w0", "a0", "kk", "ka", "rk", "lw", "lb")}
    tok = [k.vec("rwkv", cols[:, 0:off], "rwkv")]
    names["nm"] = off
    col = lambda name, i: cols[:, names[name] + i:names[name] + i + 1]
    tok.append(v.ts(cols[:, off:off + 13], cols[:, 0:13], -1.0, 1.0, ALU.mult, ALU.add, *tok))
    tok.append(v.ts(cols[:, names["w0"]:names["w0"] + 8], cols[:, names["w0"]:names["w0"] + 8], 0.5, None, ALU.mult,
                    None, *tok))
    tok.append(k.load("up", up[0:64, :], k.ins["rwkv_w_up_2"][0]))
    tok.append(k.load("up2", up[64:128, :], k.ins["rwkv_a_up_2"][0]))
    k.load_table("delta")
    ring = lambda n, w=GD: Ring([room(w) for _ in range(n)])
    shift = {n: ring(1, GD + 1) for n in "rkv"}
    shift["w"] = ring(1, G + 1)

    def mixed(kind, bank, mm, j, first, out, *w, n=GD):
        s = shift[kind].take()
        if first:
            x = a.act(s.ap[:, 0:1], cols[:, 0:1], ACT.Copy, *s.was, *tok, scale=0.0)
        else:
            x = a.act(s.ap[:, 0:1], s.ap[:, n:n + 1], ACT.Copy, *s.was)
        y = a.act(s.ap[:, 1:n + 1], bank.ap[:, 0:n], ACT.Identity, mm, x, scale=col("mu", j))
        z = v.stt(out, bank.ap[:, 0:n], col("nm", j), s.ap[:, 0:n], ALU.mult, ALU.add, y, x, *tok, *w)
        s.free = (z,)
        return z

    was = []
    for g in range(NG):
        b = fb.take()
        mm = k.project_now(b, first_wv[:, 0], 0, g, got_wa)
        sl = slice(g * G, (g + 1) * G)
        t = mixed("w", b, mm, 12, g == 0, wa[:, sl], n=G)
        b.free = (t,)
        t2 = a.act(wa[0:64, sl], wa[0:64, sl], ACT.Tanh, t)
        was.append((t, t2))
    first_w.free = (mm,)
    own = {"r": ring(2), "k": ring(2), "gl": ring(2), "av": ring(2)}
    ar_r = ring(3, 2 * GD)
    hand = {"v": ring(3), "beta": ring(2), "kappa": ring(2), "z": ring(5), "bon": ring(4), "eb": ring(4)}
    own |= {n: ring(1) for n in ("b", "kk", "kp")}
    tmp, th_r = ring(4), ring(3)
    m_r, xz_r, rhs_r, tm_r = ring(2, 8 * P), ring(2, 4 * P), ring(2, 2 * P), ring(2, 3 * P)
    t1_r = [ring(1, 2 * P), ring(1, 2 * P)]
    wu_r = ring(1, 2 * P)
    gt_r, bu_r, rp_r, yi_r = ring(2), ring(2), ring(2), ring(2)
    y_r, sq_r = ring(1), ring(1)
    state = ring(4, CH)
    c_ln = float(np.exp(-0.5)) / 2
    gated, made, scored, solved = {}, {}, {}, {}

    def load_pair(p):
        w = wr.take()
        wv = w.ap.rearrange("p (i c n) -> p i c n", i=4, c=KC)
        gw = [k.load(f"wd{i}", wv[:, i], k.weights("", w_in, c0 + p * P, P), *w.was)
              for i, c0 in enumerate((RW_R, RW_K, RW_V, RW_Z))]
        return w, wv, gw

    def front(p, g, pair):
        w, wv, gw = pair
        cs = slice(g * GD, (g + 1) * GD)
        ths = []
        for i, name in enumerate(("w0", "a0")):
            b, th = fb.take(), th_r.take()
            rows = slice(64 * i, 64 * i + 64)
            pe.wait(*was[g * GD // G], *tok, *b.was)
            mm = pe.inc(nc.tensor.matmul(b.ap[:, 0:GD], up[rows, p * P:(p + 1) * P], wa[rows, cs],
                                         start=True, stop=True))
            x = k.tanh(th.ap, b.ap[:, 0:GD], mm, *th.was, scale=0.5, bias=col(name, p))
            b.free = (x,)
            ths.append((th, x))
        for _ in range(4):
            yield
        z = hand["z"].take()
        b = fb.take()
        mm = yield from k.project(b, wv[:, 3], 0, g, gw[3], width=GD)
        gl, av = own["gl"].take(), own["av"].take()
        gl_ok = v.ts(gl.ap, ths[0][0].ap, -c_ln, -c_ln, ALU.mult, ALU.add, ths[0][1], *gl.was)
        av_ok = v.ts(av.ap, ths[1][0].ap, 0.5, 0.5, ALU.mult, ALU.add, ths[1][1], *av.was)
        ths[0][0].free, ths[1][0].free = (gl_ok,), (av_ok,)
        th = th_r.take()
        x = k.tanh(th.ap, b.ap[:, 0:GD], mm, *th.was, scale=0.5)
        yield
        z_ok = v.stt(z.ap, th.ap, 1.0, b.ap[:, 0:GD], ALU.add, ALU.mult, x, *z.was)
        b.free, th.free = (z_ok,), (z_ok,)
        yield
        r, kf, vf = own["r"].take(), own["k"].take(), hand["v"].take()
        oks = []
        for i, (kind, dst) in enumerate((("r", r), ("k", kf), ("v", vf))):
            b = fb.take()
            mm = yield from k.project(b, wv[:, i], 0, g, gw[i], width=GD)
            ok = mixed(kind, b, mm, 4 * i + p, g == 0, dst.ap, *dst.was)
            b.free = (ok,)
            oks.append(ok)
            yield
        r_ok, k_ok, v_ok = oks
        if g == ND - 1:
            w.free = (mm,)
        gated[p, g] = (r, r_ok, kf, k_ok, vf, v_ok, z, z_ok, gl, gl_ok, av, av_ok)
        yield

    def factors(p, g):
        r, r_ok, kf, k_ok, vf, v_ok, z, z_ok, gl, gl_ok, av, av_ok = gated.pop((p, g))
        bcum = own["b"].take()
        v.wait(gl_ok, *bcum.was)
        b_ok = v.inc(nc.vector.tensor_tensor_scan(out=bcum.ap, data0=cst("run64"), data1=gl.ap, initial=0.0,
                                                  op0=ALU.mult, op1=ALU.add))
        kk = own["kk"].take()
        kk0 = v.ts(kk.ap, kf.ap, col("kk", p), None, ALU.mult, None, k_ok, *kk.was)
        sq = tmp.take()
        x = a.act(sq.ap, kk.ap, ACT.Square, kk0, *sq.was)
        yield
        yield
        b = cb.take()
        pe.wait(x, *b.was)
        mm = pe.inc(nc.tensor.matmul(b.ap[:, 0:GD], k.c("head_ones"), sq.ap, start=True, stop=True))
        x = v.ts(sq.ap, b.ap[:, 0:GD], 1e-24, 2.0 ** 18, ALU.max, ALU.mult, mm)
        b.free = (x,)
        x = k.ln(sq.ap, sq.ap, x)
        norm_ok = a.act(sq.ap, sq.ap, ACT.Exp, x, scale=-0.5, bias=k.eps_col(NINE_LN2))
        kp, t = own["kp"].take(), tmp.take()
        x = v.ts(t.ap, av.ap, -1.0, col("ka", p), ALU.add, ALU.mult, av_ok, *t.was)
        kp_ok = v.stt(kp.ap, t.ap, 1.0, kf.ap, ALU.add, ALU.mult, x, k_ok, *kp.was)
        t.free, kf.free = (kp_ok,), (kp_ok,)
        yield
        kk_ok = v.tt(kk.ap, kk.ap, sq.ap, ALU.mult, norm_ok, kk0)
        sq.free = (kk_ok,)
        bn, t = hand["bon"].take(), tmp.take()
        x = v.stt(t.ap, r.ap, col("rk", p), kp.ap, ALU.mult, ALU.mult, r_ok, kp_ok, *t.was)
        yield
        yield
        b = cb.take()
        pe.wait(x, *b.was)
        mm = pe.inc(nc.tensor.matmul(b.ap[:, 0:GD], k.c("head_ones"), t.ap, start=True, stop=True))
        t.free = (mm,)
        bn_ok = v.tt(bn.ap, b.ap[:, 0:GD], vf.ap, ALU.mult, mm, v_ok, *bn.was)
        b.free = (bn_ok,)
        ar, beta, kappa, eb = ar_r.take(), hand["beta"].take(), hand["kappa"].take(), hand["eb"].take()
        ar3 = ar.ap.rearrange("p (m t) -> p m t", m=2)
        t = tmp.take()
        x = pool.tt(t.ap, bcum.ap, gl.ap, ALU.subtract, b_ok, gl_ok, *t.was)
        gl.free = (x, b_ok)
        x = a.act(t.ap, t.ap, ACT.Exp, x)
        al_ok = v.stt(ar3[:, 0, :], kk.ap, -1.0, t.ap, ALU.mult, ALU.mult, x, kk_ok, *ar.was)
        t.free = (al_ok,)
        e_ok = a.act(eb.ap, bcum.ap, ACT.Exp, b_ok, *eb.was)
        rho_ok = v.tt(ar3[:, 1, :], r.ap, eb.ap, ALU.mult, e_ok, r_ok)
        r.free = (rho_ok,)
        t = tmp.take()
        x = a.act(t.ap, bcum.ap, ACT.Exp, b_ok, *t.was, scale=-1.0)
        bcum.free = (x,)
        y = pool.tt(beta.ap, kk.ap, av.ap, ALU.mult, kk_ok, av_ok, *beta.was)
        kk.free, av.free = (y, al_ok), (y,)
        be_ok = v.tt(beta.ap, beta.ap, t.ap, ALU.mult, x, y)
        ka_ok = v.tt(kappa.ap, kp.ap, t.ap, ALU.mult, x, kp_ok, *kappa.was)
        kp.free, t.free = (ka_ok,), (ka_ok, be_ok)
        made[p, g] = dict(ar=ar, ar3=ar3, beta=beta, kappa=kappa, eb=eb, vf=vf, z=z, bn=bn, al_ok=al_ok,
                          rho_ok=rho_ok, be_ok=be_ok, ka_ok=ka_ok, e_ok=e_ok, v_ok=v_ok, z_ok=z_ok, bn_ok=bn_ok)
        yield

    half = lambda i: slice(64 * i, 64 * i + 64)
    by_h = lambda ap: ap.rearrange("p (h n) -> p h n", h=2)

    def halve(l, m4, m_ok, xz4, x_ok, t1_r, banks):
        b, t1 = banks.take(), t1_r.take()
        t13 = by_h(t1.ap)
        pe.wait(x_ok, m_ok, *b.was)
        for h in range(2):
            ins = nc.tensor.matmul(b.ap[:, h * P:(h + 1) * P], m4[:, h, 0, :], xz4[:, h, 0, :], start=True, stop=True)
        mm = pe.inc(ins)
        t_ok = v.tt(t13, by_h(b.ap[:, 0:2 * P]), bc(cst(f"low{l}"), 1, 2), ALU.mult, mm, *t1.was)
        b.free = (t_ok,)
        yield
        b = banks.take()
        b4 = b.ap.rearrange("p (h m n) -> p h m n", h=2, m=2)
        last = l == 5
        pe.wait(t_ok, *b.was)
        for h in range(2):
            if not last:
                nc.tensor.matmul(b4[:, h, 0, :], xz4[:, h, 1, :], t13[:, h, :], start=True, stop=True)
            ins = nc.tensor.matmul(b4[:, h, 1, :], t13[:, h, :], xz4[:, h, 1, :], start=True, stop=True)
        mm = pe.inc(ins)
        t1.free = (mm,)
        if last:
            x_ok = v.tt(xz4[:, :, 1, :], xz4[:, :, 1, :], b4[:, :, 1, :], ALU.add, mm)
        else:
            x_ok = v.tt(xz4, xz4, b4, ALU.add, mm)
        b.free = (x_ok,)
        yield
        return x_ok

    def scores(p, g):
        f = made[p, g]
        ar3, beta, kappa = f["ar3"], f["beta"], f["kappa"]
        rh, tm = rhs_r.take(), tm_r.take()
        b = sb.take()
        pe.wait(f["al_ok"], f["be_ok"], f["ka_ok"], f["v_ok"], *b.was)
        for i, src in enumerate((ar3[:, 0, :], beta.ap, kappa.ap, f["vf"].ap)):
            ins = nc.tensor.transpose(b.ap[:, i * P:(i + 1) * P], src, k.c("ident"))
        tr = pe.inc(ins)
        a_tm = a.act(by_h(rh.ap)[:, :, 0:64], by_h(b.ap[:, 0:P]), ACT.Copy, tr, *rh.was)
        tm_ok = a.act(tm.ap, b.ap[:, P:4 * P], ACT.Copy, tr, *tm.was)
        b.free = (tm_ok,)
        f["vf"].free = (tr, f["bn_ok"])
        yield
        m, xz = m_r.take(), xz_r.take()
        m4 = m.ap.rearrange("p (h m n) -> p h m n", h=2, m=4)
        xz4 = xz.ap.rearrange("p (h m n) -> p h m n", h=2, m=2)
        b2 = [sb.take(), sb.take()]
        pe.wait(f["rho_ok"], *b2[0].was, *b2[1].was)
        for i, src in enumerate((beta, kappa)):
            for h in range(2):
                ins = nc.tensor.matmul(b2[h].ap[:, i * 256:(i + 1) * 256], src.ap[half(h), :], ar3[half(h), :, :],
                                       start=True, stop=True)
        mm = pe.inc(ins)
        for h in range(2):
            m_ok = v.tt(m.ap.rearrange("p (h i n) -> p h i n", h=2, i=2)[:, h],
                        b2[h].ap.rearrange("p (i n) -> p i n", i=2), bc(cst("strict_incl"), 1, 2), ALU.mult, mm, *m.was)
            b2[h].free = (m_ok,)
        yield
        b2 = [sb.take(), sb.take()]
        pe.wait(*b2[0].was, *b2[1].was)
        for h in range(2):
            ins = nc.tensor.matmul(b2[h].ap[:, 0:P], ar3[half(h), 0, :], beta.ap[half(h), :], start=True, stop=True)
        mm = pe.inc(ins)
        beta.free, kappa.free = (mm,), (mm,)
        for h in range(2):
            x1 = v.tt(xz4[:, h, 0, :], b2[h].ap[:, 0:P], cst("low0"), ALU.mult, mm, *xz.was)
            b2[h].free = (x1,)
        x2 = v.tt(xz4[:, :, 1, :], m4[:, :, 0, :], bc(cst("up0"), 1, 2), ALU.mult, m_ok)
        xzf = xz.ap.rearrange("p (n j) -> p n j", j=P)
        x_ok = v.tt(xzf, xzf, bc(k.c("ident"), 1, 4), ALU.add, x1, x2)
        yield
        for l in (1, 2):
            x_ok = yield from halve(l, m4, m_ok, xz4, x_ok, t1_r[0], sb)
        scored[p, g] = (m, m4, m_ok, xz, xz4, x_ok, rh, a_tm, tm, tm_ok, tr)

    def solve(p, g):
        f = made[p, g]
        m, m4, m_ok, xz, xz4, x_ok, rh, a_tm, tm, tm_ok, tr = scored.pop((p, g))
        ar, ar3, eb = f["ar"], f["ar3"], f["eb"]
        rh3 = by_h(rh.ap)
        beta_tm, kappa_tm, v_tm = (tm.ap[:, i * P:(i + 1) * P] for i in range(3))
        b = vb.take()
        pe.wait(m_ok, tm_ok, *b.was)
        for h in range(2):
            ins = nc.tensor.matmul(b.ap[:, h * CH:(h + 1) * CH], m4[:, h, 2, :], v_tm[:, half(h)],
                                   start=True, stop=True)
        mm = pe.inc(ins)
        lk = a.act(rh3[:, :, 64:128], by_h(b.ap[:, 0:P]), ACT.Copy, mm)
        b.free = (lk,)
        yield
        for l in (3, 4, 5):
            x_ok = yield from halve(l, m4, m_ok, xz4, x_ok, t1_r[1], vb)
        wu = wu_r.take()
        wu3 = by_h(wu.ap)
        b = vb.take()
        pe.wait(lk, a_tm, x_ok, *b.was)
        for h in range(2):
            ins = nc.tensor.matmul(b.ap[:, h * P:(h + 1) * P], xz4[:, h, 1, :], rh3[:, h, :], start=True, stop=True)
        mm = pe.inc(ins)
        xz.free, rh.free = (mm, x_ok), (mm,)
        w_ok = a.act(wu.ap, b.ap[:, 0:2 * P], ACT.Copy, mm, *wu.was)
        b.free = (w_ok,)
        yield
        b2 = [vb.take(), vb.take()]
        pe.wait(w_ok, *b2[0].was, *b2[1].was)
        for h in range(2):
            for c in range(2):
                bk = b2[c].ap
                nc.tensor.matmul(bk[half(h), 0:CH], wu3[half(c), h, 0:64], beta_tm[half(c), half(h)],
                                 start=True, stop=True)
                nc.tensor.matmul(bk[half(h), CH:P], beta_tm[half(c), half(h)], wu3[half(c), h, 64:128],
                                 start=True, stop=False)
                ins = nc.tensor.matmul(bk[half(h), CH:P], kappa_tm[half(c), half(h)], v_tm[half(c), half(h)],
                                       start=False, stop=True)
        mm = pe.inc(ins)
        gt, bu = gt_r.take(), bu_r.take()
        for c in range(2):
            g_ok = v.tt(by_h(gt.ap)[:, c, :], b2[c].ap[:, 0:CH], cst("eye64"), ALU.add, mm, *gt.was)
            e = eb.ap[:, c * CH + CH - 1:(c + 1) * CH]
            u_ok = v.ts(by_h(bu.ap)[:, c, :], b2[c].ap[:, CH:P], e, None, ALU.mult, None, f["e_ok"], *bu.was)
            b2[c].free = (u_ok, g_ok)
        yield
        rp, yi = rp_r.take(), yi_r.take()
        b = vb.take()
        pe.wait(*b.was)
        for h in range(2):
            nc.tensor.matmul(b.ap[half(h), 0:P], wu3[:, h, 0:64], m4[:, h, 1, :], start=True, stop=True)
            nc.tensor.matmul(b.ap[half(h), P:2 * P], wu3[:, h, 64:128], m4[:, h, 1, :], start=True, stop=False)
            ins = nc.tensor.matmul(b.ap[half(h), P:2 * P], v_tm[:, half(h)], m4[:, h, 3, :], start=False, stop=True)
        mm = pe.inc(ins)
        rp_ok = v.tt(rp.ap, ar3[:, 1, :], b.ap[:, 0:P], ALU.add, mm, f["rho_ok"], *rp.was)
        yi_ok = a.act(yi.ap, b.ap[:, P:2 * P], ACT.Copy, rp_ok, *yi.was)
        b.free = (yi_ok,)
        m.free, tm.free, wu.free, ar.free = (mm, x_ok), (mm,), (mm,), (mm, tr, rp_ok)
        solved[p, g] = (gt, g_ok, bu, u_ok, rp, rp_ok, yi, yi_ok)
        yield

    carried = {}

    def carry(p, g):
        f = made.pop((p, g))
        gt, g_ok, bu, u_ok, rp, rp_ok, yi, yi_ok = solved.pop((p, g))
        eb = f["eb"]
        gt3, bu3 = by_h(gt.ap), by_h(bu.ap)
        if g == 0:
            s = state.take()
            v.wait(*s.was)
            carried[p] = (s, v.inc(nc.vector.memset(s.ap, 0.0)))
        states = [carried[p]]
        for c in range(2):
            old, s_ok = states[-1]
            b, new = cb.take(), state.take()
            pe.wait(s_ok, g_ok, *b.was)
            for h in range(2):
                ins = nc.tensor.matmul(b.ap[half(h), 0:CH], gt3[half(h), c, :], old.ap[half(h), :],
                                       start=True, stop=True)
            mm = pe.inc(ins)
            s_ok = v.stt(new.ap, b.ap[:, 0:CH], eb.ap[:, c * CH + CH - 1:(c + 1) * CH], bu3[:, c, :],
                         ALU.mult, ALU.add, mm, u_ok, *new.was)
            b.free = (s_ok,)
            states.append((new, s_ok))
            yield
        gt.free, bu.free, eb.free = (mm,), (s_ok,), (s_ok, f["rho_ok"])
        carried[p] = states[2]
        b = cb.take()
        pe.wait(rp_ok, states[1][1], *b.was)
        for c in range(2):
            for h in range(2):
                ins = nc.tensor.matmul(b.ap[half(h), c * CH:(c + 1) * CH], states[c][0].ap[half(h), :],
                                       rp.ap[half(h), c * CH:(c + 1) * CH], start=True, stop=True)
        mm = pe.inc(ins)
        rp.free = (mm,)
        states[0][0].free, states[1][0].free = (mm,), (mm,)
        if g == ND - 1:
            states[2][0].free = (s_ok,)
        y = y_r.take()
        y_ok = v.tt(y.ap, b.ap[:, 0:GD], yi.ap, ALU.add, mm, yi_ok, *y.was)
        b.free, yi.free = (y_ok,), (y_ok,)
        yield
        b = cb.take()
        pe.wait(y_ok, *b.was)
        mm = pe.inc(nc.tensor.matmul(b.ap[:, 0:GD], k.c("head_ones"), y.ap, start=True, stop=True))
        x = v.stt(y.ap, b.ap[:, 0:GD], -1.0 / HD, y.ap, ALU.mult, ALU.add, mm)
        b.free = (x,)
        sq = sq_r.take()
        x2 = a.act(sq.ap, y.ap, ACT.Square, x, *sq.was)
        yield
        b = cb.take()
        pe.wait(x2, *b.was)
        mm = pe.inc(nc.tensor.matmul(b.ap[:, 0:GD], k.c("head_ones"), sq.ap, start=True, stop=True))
        x2 = k.ln(sq.ap, b.ap[:, 0:GD], mm, scale=1.0 / HD, bias=k.eps_col(GN_EPS))
        b.free = (x2,)
        x2 = a.act(sq.ap, sq.ap, ACT.Exp, x2, scale=-0.5)
        x = v.tt(y.ap, y.ap, sq.ap, ALU.mult, x, x2)
        sq.free = (x,)
        x = v.ts(y.ap, y.ap, col("lw", p), col("lb", p), ALU.mult, ALU.add, x)
        x = v.tt(y.ap, y.ap, f["bn"].ap, ALU.add, x, f["bn_ok"])
        f["bn"].free = (x,)
        x = v.stt(k.oT[:, 4 + p, g * GD:(g + 1) * GD], y.ap, 0.5, f["z"].ap, ALU.mult, ALU.mult, x, f["z_ok"])
        y.free, f["z"].free = (x,), (x,)
        yield

    groups = [(p, g) for p in range(4) for g in range(ND)]
    pairs = {}
    for i in range(len(groups) + 4):
        at = lambda back: groups[i - back] if 0 <= i - back < len(groups) else None
        ahead = None
        if at(0):
            p, g = at(0)
            if g == 0:
                pairs[p] = load_pair(p)
            ahead = front(p, g, pairs[p])
        interleave(("carry", carry(*at(4)) if at(4) else None), ("solve", solve(*at(3)) if at(3) else None),
                   ("scores", scores(*at(2)) if at(2) else None), ("factors", factors(*at(1)) if at(1) else None),
                   ("front", ahead))


def build(nc, ins, out, x1, x2, spans, at):
    with ExitStack() as ctx:
        k = Core(nc, ctx, ins, spans, at)
        k.load_constants()
        x0 = ins["x"][0]
        attention(k)
        attention_gate(k)
        finish_layer(k, 0, x0, x1, ins["attn_w_out"][0], ins["attn_b_out"][0], ins["post_norm_w"][0],
                     "pre1", None)
        recurrence(k)
        finish_layer(k, 1, x1, x2, ins["rec_w_out"][0], None, ins["post_norm_w"][1], "norm2", None)
        gla(k)
        delta_rule(k)
        finish_layer(k, 2, x2, out, ins["w_out_2"][0], None, None, None, ins["final_norm_w_2"])
        k.sp.wait(*k.dma.stores)


_INS = ["x", "pre_norm_w", "post_norm_w", "attn_w_in", "attn_b_in", "attn_sinks", "attn_w_out",
        "attn_b_out", "rec_w_in", "rec_lb_logits", "rec_gnorm_w", "rec_w_out", "norm_w_2", "w_in_2",
        "gla_gate_up_2", "gla_gate_bias_2", "gla_norm_w_2", "rwkv_mu_2", "rwkv_w0_2", "rwkv_w_up_2", "rwkv_a0_2",
        "rwkv_a_up_2", "rwkv_k_k_2", "rwkv_k_a_2", "rwkv_r_k_2", "rwkv_ln_w_2", "rwkv_ln_b_2", "w_out_2",
        "final_norm_w_2"]


def kernel(**inputs):
    import concourse.bacc as _bacc
    from concourse.bass_utils import run_bass_kernel_spmd as _run

    nc = _bacc.Bacc("TRN2", target_bir_lowering=False, num_devices=1, dynamic_dma_scratch_size=1024)
    table, spans, at, select = constant_tables()
    arrays, ins = {}, {}
    for name in _INS:
        a = np.ascontiguousarray(inputs[name])
        arrays[f"in_{name}"] = a
        ins[name] = nc.dram_tensor(f"in_{name}", a.shape, mybir.dt.from_np(a.dtype), kind="ExternalInput").ap()
    positions = np.ascontiguousarray(np.asarray(inputs["positions"]).reshape(NT, P).T)
    for name, a in (("table", table), ("select", select), ("columns", feature_columns(inputs)),
                    ("positions", positions)):
        arrays[name] = a
        ins[name] = nc.dram_tensor(name, a.shape, mybir.dt.from_np(a.dtype), kind="ExternalInput").ap()
    out = nc.dram_tensor("out", (1, T, D), F32, kind="ExternalOutput").ap()
    x1 = nc.dram_tensor("x_after_0", (T, D), F32, kind="Internal").ap()
    x2 = nc.dram_tensor("x_after_1", (T, D), F32, kind="Internal").ap()
    build(nc, ins, out[0], x1, x2, spans, at)
    r = _run(nc, [arrays], core_ids=[0])
    return r.results[0]["out"]
```
